# Optimizing a Trainium2 kernel written in Bass

```python
import math
import jax, jax.numpy as jnp
from jax import lax
import numpy as np

D_MODEL = 1024
BATCH = 1
SEQ = 2048
DEPTH = 1
DEC_BATCH = 8
DEC_SEQ = 1
PAST_LEN = 8192
PAGE_SIZE = 128

N_META = 16
D_MIX = D_MODEL
D_REC = D_MIX // 2
D_ATT = D_MIX - D_REC
REC_HEAD_DIM = 128
N_REC_HEADS = D_REC // REC_HEAD_DIM
ATT_HEAD_DIM = 64
N_ATT_HEADS = D_ATT // (2 * ATT_HEAD_DIM)
D_IN = 4 * D_REC + 4 * D_ATT
CHUNK = 64
Q_BLOCK = 128
EPS = 1e-6

kernel_name = "hymba_hgrn2_diffattn_step"

F32 = jnp.float32

def rms_norm(x, w):
    xf = x.astype(F32)
    y = xf * lax.rsqrt(jnp.mean(xf * xf, axis=-1, keepdims=True) + EPS)
    return (y * w.astype(F32)).astype(x.dtype)

def lower_bounds(lb_logits):
    p = jax.nn.softmax(lb_logits.astype(F32), axis=0)
    c = jnp.cumsum(p, axis=0)
    return c - c[0:1]

def hgrn2_chunk(S, inp):
    q, k, v, g = inp
    C = q.shape[2]
    b = jnp.cumsum(g, axis=2)
    causal = jnp.tril(jnp.ones((C, C), dtype=bool))
    diff = b[:, :, :, None, :] - b[:, :, None, :, :]
    decay = jnp.exp(jnp.where(causal[None, None, :, :, None], diff, -jnp.inf))
    a = jnp.einsum('bhtc,bhsc,bhtsc->bhts', q, k, decay)
    o = (jnp.einsum('bhts,bhsv->bhtv', a, v)
         + jnp.einsum('bhtc,bhcv->bhtv', q * jnp.exp(b), S))
    b_last = b[:, :, -1:, :]
    S_new = (jnp.exp(b_last[:, :, 0, :])[..., None] * S
             + jnp.einsum('bhsc,bhsv->bhcv', k * jnp.exp(b_last - b), v))
    return S_new, o

def hgrn2_scan(q, k, v, g, S0):
    B, H, T, _ = q.shape
    c = min(CHUNK, T)
    n = -(-T // c)
    pad = n * c - T

    def prep(a):
        a = jnp.pad(a, ((0, 0), (0, 0), (0, pad), (0, 0)))
        return jnp.moveaxis(a.reshape(B, H, n, c, a.shape[-1]), 2, 0)

    S, o = lax.scan(hgrn2_chunk, S0.astype(F32), (prep(q), prep(k), prep(v), prep(g)))
    o = jnp.moveaxis(o, 0, 2).reshape(B, H, n * c, -1)[:, :, :T]
    return o, S.astype(S0.dtype)

def diff_attention(q, k, v, q_pos, k_pos, lam):
    B, Tq, H, _, Dh = q.shape
    bq = min(Q_BLOCK, Tq)
    n = -(-Tq // bq)
    pad = n * bq - Tq
    qp = jnp.pad(q, ((0, 0), (0, pad), (0, 0), (0, 0), (0, 0)))
    posp = jnp.pad(q_pos, (0, pad), mode='edge')
    qb = jnp.moveaxis(qp.reshape(B, n, bq, H, 2, Dh), 1, 0)
    pb = posp.reshape(n, bq)
    kf = k.astype(F32)
    vf = v.astype(F32)
    scale = Dh ** -0.5

    def block(args):
        qi, pi = args
        s = jnp.einsum('bqhcd,bkhcd->bhcqk', qi.astype(F32), kf) * scale
        mask = k_pos[None, :] <= pi[:, None]
        p = jax.nn.softmax(jnp.where(mask, s, -jnp.inf), axis=-1)
        a = p[:, :, 0] - lam * p[:, :, 1]
        return jnp.einsum('bhqk,bkhv->bqhv', a, vf)

    o = lax.map(block, (qb, pb))
    return jnp.moveaxis(o, 0, 1).reshape(B, n * bq, H, -1)[:, :Tq]

def mixer_layer(h, l, S0, k_past, v_past, front_pad, norm_w, w_in, w_out, lb,
                hgrn_norm_w, subln_w, lam_q1, lam_k1, lam_q2, lam_k2):
    B, T, _ = h.shape
    xn = rms_norm(h, norm_w[l])
    proj = jnp.einsum('btd,de->bte', xn, w_in[l])
    rq, rf, ri, rg, aq, ak, av, ag = jnp.split(
        proj, [D_REC, 2 * D_REC, 3 * D_REC, 4 * D_REC, 4 * D_REC + D_ATT,
               4 * D_REC + 2 * D_ATT, 4 * D_REC + 3 * D_ATT], axis=-1)

    lbl = lb[l]
    zf = rf.astype(F32)
    log_f = jnp.logaddexp(jnp.log(lbl), jnp.log1p(-lbl) + jax.nn.log_sigmoid(zf))
    k_in = (1.0 - lbl) * jax.nn.sigmoid(-zf)

    def rec_heads(a):
        a = a.astype(F32).reshape(B, T, N_REC_HEADS, REC_HEAD_DIM).transpose(0, 2, 1, 3)
        return jnp.pad(a, ((0, 0), (0, 0), (front_pad, 0), (0, 0)))

    o_rec, S_new = hgrn2_scan(rec_heads(rq), rec_heads(k_in), rec_heads(ri), rec_heads(log_f), S0)
    o_rec = o_rec[:, :, front_pad:].transpose(0, 2, 1, 3)
    o_rec = rms_norm(o_rec, hgrn_norm_w[l]).reshape(B, T, D_REC)
    y_rec = (o_rec * jax.nn.silu(rg.astype(F32))).astype(h.dtype)

    q = aq.reshape(B, T, N_ATT_HEADS, 2, ATT_HEAD_DIM)
    k_new = ak.reshape(B, T, N_ATT_HEADS, 2 * ATT_HEAD_DIM)
    v_new = av.reshape(B, T, N_ATT_HEADS, 2 * ATT_HEAD_DIM)
    if k_past is None:
        k_all, v_all, P = k_new, v_new, 0
    else:
        P = k_past.shape[1]
        k_all = jnp.concatenate([k_past.astype(k_new.dtype), k_new], axis=1)
        v_all = jnp.concatenate([v_past.astype(v_new.dtype), v_new], axis=1)
    q_pos = P + jnp.arange(T, dtype=jnp.int32)
    k_pos = jnp.arange(P + T, dtype=jnp.int32)
    lam_init = 0.8 - 0.6 * math.exp(-0.3 * l)
    lam = (jnp.exp(jnp.sum(lam_q1[l].astype(F32) * lam_k1[l].astype(F32)))
           - jnp.exp(jnp.sum(lam_q2[l].astype(F32) * lam_k2[l].astype(F32))) + lam_init)
    o_att = diff_attention(q, k_all.reshape(B, P + T, N_ATT_HEADS, 2, ATT_HEAD_DIM),
                           v_all, q_pos, k_pos, lam)
    o_att = rms_norm(o_att, subln_w[l]) * (1.0 - lam_init)
    y_att = (o_att.reshape(B, T, D_ATT) * jax.nn.silu(ag.astype(F32))).astype(h.dtype)

    out = jnp.einsum('bte,ed->btd', jnp.concatenate([y_rec, y_att], axis=-1), w_out[l])
    return h + out, S_new, k_new, v_new

def setup_inputs(seed: int = 0) -> dict:
    key = jax.random.key(seed)
    ks = jax.random.split(key, 20)
    n_pages = PAST_LEN // PAGE_SIZE
    n_used = DEC_BATCH * n_pages
    n_phys = n_used + max(1, n_used // 4)
    kv_shape = (DEPTH, n_phys, PAGE_SIZE, N_ATT_HEADS, 2 * ATT_HEAD_DIM)
    nrm = lambda k, s: jax.random.normal(k, s, F32)
    return {
        "x_prompt": nrm(ks[0], (BATCH, SEQ, D_MODEL)),
        "x_sample": nrm(ks[1], (DEC_BATCH, DEC_SEQ, D_MODEL)),
        "cache_k": nrm(ks[2], kv_shape),
        "cache_v": nrm(ks[3], kv_shape),
        "state_hgrn": 0.3 * nrm(ks[4], (DEPTH, DEC_BATCH, N_REC_HEADS, REC_HEAD_DIM, REC_HEAD_DIM)),
        "page_table": jax.random.permutation(ks[5], n_phys)[:n_used].reshape(DEC_BATCH, n_pages).astype(jnp.int32),
        "meta_tokens": nrm(ks[6], (N_META, D_MODEL)),
        "norm_w": 1.0 + 0.02 * nrm(ks[7], (DEPTH, D_MODEL)),
        "w_in": nrm(ks[8], (DEPTH, D_MODEL, D_IN)) * D_MODEL ** -0.5,
        "w_out": nrm(ks[9], (DEPTH, D_MIX, D_MODEL)) * D_MIX ** -0.5,
        "lb_logits": nrm(ks[10], (DEPTH, D_REC)),
        "hgrn_norm_w": 1.0 + 0.02 * nrm(ks[11], (DEPTH, REC_HEAD_DIM)),
        "subln_w": 1.0 + 0.02 * nrm(ks[12], (DEPTH, 2 * ATT_HEAD_DIM)),
        "lam_q1": 0.1 * nrm(ks[13], (DEPTH, ATT_HEAD_DIM)),
        "lam_k1": 0.1 * nrm(ks[14], (DEPTH, ATT_HEAD_DIM)),
        "lam_q2": 0.1 * nrm(ks[15], (DEPTH, ATT_HEAD_DIM)),
        "lam_k2": 0.1 * nrm(ks[16], (DEPTH, ATT_HEAD_DIM)),
        "final_norm_w": 1.0 + 0.02 * nrm(ks[17], (D_MODEL,)),
    }

def reference(x_prompt, x_sample, cache_k, cache_v, state_hgrn, page_table, meta_tokens,
              norm_w, w_in, w_out, lb_logits, hgrn_norm_w, subln_w,
              lam_q1, lam_k1, lam_q2, lam_k2, final_norm_w):
    lb = lower_bounds(lb_logits)
    n_seq, n_pages = page_table.shape
    front_pad = (-N_META) % CHUNK
    bp = x_prompt.shape[0]
    meta = jnp.broadcast_to(meta_tokens[None].astype(x_prompt.dtype), (bp, N_META, D_MODEL))
    hp = jnp.concatenate([meta, x_prompt], axis=1)
    hs = x_sample
    kp, vp, sp, ksm, vsm, ssm = [], [], [], [], [], []
    for l in range(DEPTH):
        S0p = jnp.zeros((bp, N_REC_HEADS, REC_HEAD_DIM, REC_HEAD_DIM), state_hgrn.dtype)
        hp, S_p, k_p, v_p = mixer_layer(hp, l, S0p, None, None, front_pad, norm_w, w_in, w_out, lb,
                                        hgrn_norm_w, subln_w, lam_q1, lam_k1, lam_q2, lam_k2)
        k_past = cache_k[l][page_table].reshape(n_seq, n_pages * PAGE_SIZE, N_ATT_HEADS, 2 * ATT_HEAD_DIM)
        v_past = cache_v[l][page_table].reshape(n_seq, n_pages * PAGE_SIZE, N_ATT_HEADS, 2 * ATT_HEAD_DIM)
        hs, S_s, k_s, v_s = mixer_layer(hs, l, state_hgrn[l], k_past, v_past, 0, norm_w, w_in, w_out, lb,
                                        hgrn_norm_w, subln_w, lam_q1, lam_k1, lam_q2, lam_k2)
        kp.append(k_p); vp.append(v_p); sp.append(S_p)
        ksm.append(k_s); vsm.append(v_s); ssm.append(S_s)
    y_prompt = rms_norm(hp, final_norm_w)[:, N_META:]
    y_sample = rms_norm(hs, final_norm_w)
    new_k_prompt = jnp.stack(kp)
    new_v_prompt = jnp.stack(vp)
    new_state_prompt = jnp.stack(sp)
    new_k_sample = jnp.stack(ksm)
    new_v_sample = jnp.stack(vsm)
    new_state_sample = jnp.stack(ssm)
    return (y_prompt, y_sample, new_k_prompt, new_v_prompt, new_state_prompt,
            new_k_sample, new_v_sample, new_state_sample)


_drawn_inputs = setup_inputs


def setup_inputs(seed=0):
    import zlib

    import numpy as np

    out = dict(_drawn_inputs(seed))
    spreads = {}
    factors = {'hgrn_norm_w': 6.942,
     'subln_w': 8.0,
     'lam_q1': 3.404,
     'lam_k1': 5.141,
     'lam_q2': 3.354,
     'lam_k2': 4.631,
     'final_norm_w': 2.874}
    for name, (base, spread) in spreads.items():
        noise = np.random.default_rng([zlib.crc32(name.encode()), seed]).standard_normal(out[name].shape)
        drawn = base * np.exp(spread * noise) if base else spread * noise
        out[name] = __import__('jax').numpy.asarray(drawn.astype(out[name].dtype))
    for name, factor in factors.items():
        out[name] = (out[name] * factor).astype(out[name].dtype)
    return out
```

```python
from contextlib import ExitStack

import concourse.bass as bass
from concourse import mybir

ALU = mybir.AluOpType
ACT = mybir.ActivationFunctionType
F32 = mybir.dt.float32
BF16 = mybir.dt.bfloat16
I32 = mybir.dt.int32
U32 = mybir.dt.uint32
X = mybir.AxisListType.X
XY = mybir.AxisListType.XY

P = 128
D = 1024
DC = D // P
G = 512
H = 4
NT = 16
NMETA = 16
NS = 8
TR = NMETA + NS
NPG = 64
HC = 2 * H
EPS = 1e-6
LAM0 = 0.8 - 0.6
BIG = 1e30
SLOTS = 8
READ = 4
RSQRT_SEED = 1597463007.0
RS_STEPS = 11


def blocks_before(g, r):
    return 16 * g * (g + 1) + r * (8 * (g + 1))


class Chain:

    def __init__(self, eng, sem):
        self.eng, self.sem, self.base, self.r, self.per, self.n, self.first = eng, sem, 0, 0, 0, 0, 0

    def enter(self, first, per):
        self.first, self.base, self.per, self.n = first, self.base - first * per, per, 0

    def leave(self, times):
        assert self.n == self.per, f"chain: {self.n} steps, declared {self.per}"
        self.base, self.r, self.per, self.n = self.base + (self.first + times) * self.n, 0, 0, 0

    def flat(self):
        self.base, self.r, self.per, self.n = self.base + self.n, 0, 0, 0

    def __call__(self, ins):
        self.n += 1
        ins.then_inc(self.sem, 1)
        self.eng.wait_ge(self.sem, self.base + self.r * self.per + self.n)


TWO_FREE = 2
FOUR_FREE = 4
ONE_ON = 1
SU_BANK = 3
OUT_SLOTS = 4


def after(value, free):
    return value + free


def need(eng, sem, value):
    if isinstance(value, int) and value <= 0:
        return
    eng.wait_ge(sem, value)


def build(nc, x_prompt, x_sample, cache_k, cache_v, state_hgrn, page_table, meta_tokens, norm_w, w_in, w_out,
          lb_logits, hgrn_norm_w, subln_w, lam_q1, lam_k1, lam_q2, lam_k2, final_norm_w,
          y_prompt, y_sample, new_k_prompt, new_v_prompt, new_state_prompt,
          new_k_sample, new_v_sample, new_state_sample):
    xp = x_prompt[0]
    xs = x_sample.rearrange("b t d -> (b t) d")
    yp = y_prompt[0]
    ys = y_sample.rearrange("b t d -> (b t) d")
    kc = cache_k[0].rearrange("g t h d -> g t (h d)")
    vc = cache_v[0].rearrange("g t h d -> g t (h d)")
    nkp = new_k_prompt[0, 0].rearrange("t h d -> t (h d)")
    nvp = new_v_prompt[0, 0].rearrange("t h d -> t (h d)")
    nks = new_k_sample[0].rearrange("b t h d -> (b t) (h d)")
    nvs = new_v_sample[0].rearrange("b t h d -> (b t) (h d)")
    pages = page_table.rearrange("b (a n) -> a (b n)", a=1)
    win = w_in[0].rearrange("(c p) n -> p c n", p=P)
    wout = w_out[0].rearrange("(c p) n -> p c n", p=P)
    s_in = state_hgrn[0].rearrange("b h c v -> c (b h) v")
    s_out = new_state_sample[0].rearrange("b h c v -> c (b h) v")
    sp_out = new_state_prompt[0, 0].rearrange("h c v -> c h v")
    y_att_dram = nc.dram_tensor("y_att_scratch", (NT, P, G), F32, kind="Internal").ap()

    with ExitStack() as ctx:
        def sb(name, shape, dt=F32):
            return ctx.enter_context(nc.sbuf_tensor(name, shape, dt))

        def sem(name):
            return ctx.enter_context(nc.semaphore(name))

        ident = sb("ident", [P, P])
        identb = sb("identb", [P, P], BF16)
        causal = sb("causal", [P, 896], BF16)
        normw = sb("normw", [P, D])
        subw = sb("subw", [P, P])
        hgw = sb("hgw", [P, P])
        ones = sb("ones", [P, P])
        pick = sb("pick", [P, 47])
        zero8 = sb("zero8", [P, 8])
        start = sb("start", [P, 14])
        hmask = sb("hmask", [P, H])
        sgn = sb("sgn", [P, 1])
        nlam = sb("nlam", [P, 1])
        lamr = sb("lamr", [P, 4, 64])
        lamw = sb("lamw", [P, 8])
        lbl = sb("lbl", [P, H])
        lbw = sb("lbw", [P, 4, H])
        selm = sb("selm", [P, NS])
        W = sb("W", [P, 4, DC, G])
        xbuf = sb("xbuf", [P, D])
        U = sb("U", [P, D])
        xT = sb("xT", [P, DC, P])
        gw = sb("gw", [P, G])
        ssx = sb("ssx", [P, 2])
        rsb = sb("rsb", [P, 3, 4])
        qX = sb("qX", [P, G])
        vX = sb("vX", [P, G])
        gwX = sb("gwX", [P, G])
        oX = sb("oX", [P, G])
        sNew = sb("sNew", [P, HC])
        Kt = sb("Kt", [P, 2, 2, G])
        Vt = sb("Vt", [P, 2, 2, G])
        qb = sb("qb", [P, G])
        sc = sb("sc", [P, 2, NPG + 1, HC])
        pst = sb("pst", [P, 16 * HC])
        mpart = sb("mpart", [P, HC])
        mx8 = sb("mx8", [HC, 1])
        mxd = sb("mxd", [HC, HC])
        psums = sb("psums", [P, HC])
        srep = sb("srep", [P, P])
        coefD = sb("coefD", [P, 2])
        tmpD = sb("tmpD", [P, G])
        Qz = sb("Qz", [P, 2, H, P])
        Pb = sb("Pb", [P, 4, G])
        P4 = sb("P4", [P, 16])
        PTs = sb("PTs", [P, 2, G])
        oh = sb("oh", [P, G])
        negm = sb("negm", [P, 2, 2])
        sums = sb("sums", [P, 2, 5])
        rcp = sb("rcp", [P, 2])
        ssO = sb("ssO", [P, H])
        KTW = H * (NT * P + NMETA)
        region = sb("region", [P, KTW + NT * G])
        KT = region[:, 0:KTW].rearrange("p (h t) -> p h t", h=H)
        V = region[:, KTW:KTW + NT * G].rearrange("p (t n) -> p t n", t=NT)
        at = [0]

        def part(n):
            at[0] += n
            assert at[0] <= KTW + NT * G
            return region[:, at[0] - n:at[0]]

        Wo = part(DC * D).rearrange("p (c n) -> p c n", c=DC)
        fw = part(D)
        ycat = part(D)
        hbuf = part(D)
        yTs = part(D).rearrange("p (c t) -> p c t", c=DC)
        masks = part(8 * P).rearrange("p (l t) -> p l t", l=8)
        S_ = part(G)
        qT = part(G)
        kT = part(G)
        PP = part(G)
        QQ = part(G)
        Xl = [part(G), sb("Xl1", [P, G])[:, :]]
        Am = sb("Am", [P, G])[:, :]
        XQ = Qz[:, 0, :, :].rearrange("p h t -> p (h t)")
        Pflat = Pb[:, :, :].rearrange("p a n -> p (a n)")
        XK = Pflat[:, 0:G]
        ib = Pflat[:, G:2 * G]
        kd = Pflat[:, 2 * G:3 * G]
        QM = Qz[:, :, :, :].rearrange("p a h t -> p (a h t)")[:, 0:H * NS * TR].rearrange("p (h n) -> p h n", h=H)
        AX = PTs[:, 0, 0:H * TR].rearrange("p (h t) -> p h t", h=H)
        qPX = PTs[:, 0, H * TR:2 * H * TR].rearrange("p (h t) -> p h t", h=H)
        fX = PTs[:, 0, 2 * H * TR:3 * H * TR].rearrange("p (h t) -> p h t", h=H)
        kX = Pflat[:, 3 * G:4 * G]
        kmX = PTs[:, 1, :]
        SX = W[:, 0, :, :].rearrange("p c n -> p (c n)").rearrange("p (s v) -> p s v", v=P)

        PS = ctx.enter_context(nc.psum_tensor("PS", [P, 4, G], F32))
        PT = ctx.enter_context(nc.psum_tensor("PT", [P, 2, G], F32))
        PO = ctx.enter_context(nc.psum_tensor("PO", [P, G], F32))
        PD = ctx.enter_context(nc.psum_tensor("PD", [P, G], F32))

        const_in = sem("const_in"); made = sem("made"); cst = sem("cst"); lam_e = sem("lam_e"); cst2 = sem("cst2")
        wA = sem("wA"); wB = sem("wB"); wO = sem("wO")
        x_loaded = sem("x_loaded"); ss_ready = sem("ss_ready"); xn_ready = sem("xn_ready")
        x_tr = sem("x_tr"); xT_ready = sem("xT_ready"); proj = sem("proj")
        q_ev = sem("q_ev"); k_ev = sem("k_ev"); v_ev = sem("v_ev"); th_ev = sem("th_ev"); g_ev = sem("g_ev")
        qk_tr = sem("qk_tr"); qT_ev = sem("qT_ev"); kT_ev = sem("kT_ev")
        k_st = sem("k_st"); v_st = sem("v_st"); 
        S_done = sem("S_done"); m_ready = sem("m_ready"); P_ready = sem("P_ready"); P_tr = sem("P_tr")
        PT_ev = sem("PT_ev"); PV_done = sem("PV_done"); post = sem("post"); ssO_ready = sem("ssO_ready")
        y_ready = sem("y_ready"); qX_tr = sem("qX_tr"); dve = sem("dve")
        k_load = [sem("k_load0"), sem("k_load1")]; v_load = [sem("v_load0"), sem("v_load1")]
        k_used = sem("k_used"); v_used = sem("v_used"); pst_ready = sem("pst_ready")
        d_om = sem("d_om"); d_cmb = sem("d_cmb"); d_mx = sem("d_mx"); d_row = sem("d_row"); d_mxT = sem("d_mxT"); d_mxd = sem("d_mxd")
        d_mb = sem("d_mb"); d_sub = sem("d_sub"); d_exp = sem("d_exp"); d_sr = sem("d_sr"); d_L = sem("d_L")
        d_qm = sem("d_qm"); d_qb = sem("d_qb"); d_end = sem("d_end"); d_v0 = sem("d_v0"); d_v1 = sem("d_v1")
        z_ev = sem("z_ev"); kf = sem("kf"); x_lev = sem("x_lev"); a_lev = sem("a_lev"); a_cp = sem("a_cp")
        kd_tr = sem("kd_tr"); kd_ev = sem("kd_ev"); o_done = sem("o_done"); su = sem("su"); s_upd = sem("s_upd")
        ssR = sem("ssR"); yB = sem("yB"); y_tr = sem("y_tr"); yT_ev = sem("yT_ev"); h_mm = sem("h_mm")
        h_add = sem("h_add"); ssH = sem("ssH"); y_out = sem("y_out"); yb_st = sem("yb_st"); ya_load = sem("ya_load")
        hx_load = sem("hx_load"); b_made = sem("b_made"); st_in = sem("st_in"); t_dve = sem("t_dve")
        t_pe = sem("t_pe"); t_act = sem("t_act"); st_out = sem("st_out"); bconst = sem("bconst"); b_init = sem("b_init")

        block = ctx.enter_context(nc.Block())
        KALL = NT + 1

        def load_x(eng, dst, s, t):
            if isinstance(t, int) and t == 0:
                eng.dma_start(dst[0:16, :], meta_tokens).then_inc(s, 16)
                eng.dma_start(dst[16:P, :], xp[0:112, :]).then_inc(s, 16)
            elif isinstance(t, int):
                eng.dma_start(dst[0:16, :], xp[t * P - 16:t * P, :]).then_inc(s, 16)
                eng.dma_start(dst[16:P, :], xp[t * P:t * P + 112, :]).then_inc(s, 16)
            else:
                eng.dma_start(dst[0:16, :], xp[bass.ds(t * P - 16, 16), :]).then_inc(s, 16)
                eng.dma_start(dst[16:P, :], xp[bass.ds(t * P, 112), :]).then_inc(s, 16)

        def load_tail(eng, dst, s):
            eng.dma_start(dst[0:16, :], xp[NT * P - 16:NT * P, :]).then_inc(s, 16)
            eng.dma_start(dst[16:TR, :], xs).then_inc(s, 16)

        @block.sync
        def _(sp):
            def page_numbers(index, count):
                _, numbers = nc.values_load_multi_w_load_instructions(
                    pages[:, bass.ds(index, count)], engines=[mybir.EngineType.SP], min_val=0, max_val=kc.shape[0] - 1)
                return numbers

            def page_pair(cache, dst, pair, s, free, uses):
                need(sp, free, uses)
                for u, page in enumerate(pair):
                    sp.dma_start(dst[:, u, :], cache[bass.ds(page, 1), :, :].rearrange("a t n -> t (a n)")).then_inc(s, 16)

            def slots(it, first, last, keys=True, values=True):
                for s0 in range(first, last, READ):
                    count = min(READ, last - s0)
                    if keys:
                        kp = page_numbers(16 * it + 2 * s0, 2 * count)
                    if values:
                        vp = page_numbers(16 * (it - 4) + 2 * s0, 2 * count)
                    for s in range(s0, s0 + count):
                        u = 2 * (s - s0)
                        if keys:
                            page_pair(kc, Kt[:, s % 2], kp[u:u + 2], k_load[s % 2], k_used, after(8 * it + (s - 1), TWO_FREE))
                        if values:
                            page_pair(vc, Vt[:, s % 2], vp[u:u + 2], v_load[s % 2], v_used,
                                      after(8 * (it - 4) + (s - 1), TWO_FREE))

            sp.wait_ge(made, 1)
            load_tail(sp, xbuf, x_loaded)
            sp.dma_start(normw[:, :], norm_w.partition_broadcast(P).rearrange("p a d -> p (a d)")).then_inc(const_in, 16)
            sp.dma_start(subw[:, :], subln_w.partition_broadcast(P).rearrange("p a d -> p (a d)")).then_inc(const_in, 16)
            sp.dma_start(hgw[:, :], hgrn_norm_w.partition_broadcast(P).rearrange("p a d -> p (a d)")).then_inc(const_in, 16)
            for n, a in enumerate((lam_q1, lam_k1, lam_q2, lam_k2)):
                sp.dma_start(lamr[:, n, :], a.partition_broadcast(P).rearrange("p a d -> p (a d)")).then_inc(const_in, 16)
            with nc.allow_non_contiguous_dma(reason="512 lower-bound logits, channel on partition"):
                sp.dma_start(lbl[:, :], lb_logits.rearrange("a (h c) -> c (a h)", c=P)).then_inc(const_in, 16)
            sp.wait_ge(xn_ready, 1)
            load_x(sp, xbuf, x_loaded, 0)
            with sp.Fori(0, 4) as it:
                need(sp, xn_ready, it + 2)
                load_x(sp, xbuf, x_loaded, it + 1)
                slots(it, 0, SLOTS, values=False)
            with sp.Fori(4, NT - 1) as it:
                need(sp, xn_ready, it + 2)
                load_x(sp, xbuf, x_loaded, it + 1)
                slots(it, 0, SLOTS)
            sp.wait_ge(xn_ready, NT + 1)
            load_x(sp, xbuf, x_loaded, 0)
            slots(NT - 1, 0, SLOTS)

            with sp.Fori(0, NT - 1) as t:
                need(sp, xn_ready, t + KALL + 1)
                load_x(sp, xbuf, x_loaded, t + 1)
                slots(t + NT, 0, SLOTS)
            sp.wait_ge(xn_ready, 2 * KALL - 1)
            load_tail(sp, xbuf, x_loaded)
            slots(2 * NT - 1, 0, SLOTS)
            slots(2 * NT, 0, 2, keys=False)
            sp.wait_ge(proj, 4 * (2 * KALL))
            sp.dma_start(SX, s_in).then_inc(st_in, 16)
            slots(2 * NT, 2, SLOTS, keys=False)
            with sp.Fori(2 * NT + 1, 2 * NT + 4) as it:
                slots(it, 0, SLOTS, keys=False)
            sp.wait_ge(t_dve, 4)
            sp.dma_start(s_out, SX).then_inc(st_out, 16)
            sp.dma_start(sp_out, S_.rearrange("p (h v) -> p h v", h=H)).then_inc(st_out, 16)
            sp.wait_ge(y_out, NT + 1)
            sp.dma_start(yp[NT * P - 16:NT * P, :], hbuf[0:16, :]).then_inc(st_out, 16)
            sp.dma_start(ys, hbuf[16:TR, :]).then_inc(st_out, 16)
            sp.wait_ge(st_out, 64)
            sp.wait_ge(k_st, 32 + 16 * NT)
            sp.wait_ge(v_st, 32 + 32 * NT)

        @block.gpsimd
        def _(pool):
            pool.memset(xbuf[:, :], 0.0).then_inc(made, 1)
            pool.memset(ident[:, :], 0.0).then_inc(made, 1)
            pool.memset(causal[:, :], 0.0).then_inc(made, 1)
            pool.wait_ge(made, 3)
            pool.affine_select(out=ident[:, :], in_=ident[:, :], compare_op=ALU.not_equal, fill=1.0, base=0,
                               pattern=[[-1, P]], channel_multiplier=1).then_inc(made, 1)
            pool.affine_select(out=causal[:, :], in_=causal[:, :], compare_op=ALU.is_ge, fill=-BIG, base=384,
                               pattern=[[-1, 896]], channel_multiplier=1).then_inc(made, 1)
            pool.memset(ones[:, :], 1.0).then_inc(made, 1)
            pool.memset(srep[:, :], 1.0).then_inc(made, 1)
            pool.memset(pick[:, :], 0.0).then_inc(made, 1)
            pool.memset(zero8[:, :], 0.0).then_inc(made, 1)
            pool.memset(Qz[:, :, :, :], 0.0).then_inc(made, 1)
            pool.wait_ge(made, 10)
            pool.memset(pick[:, 23:24], 1.0).then_inc(made, 1)
            pool.memset(region[:, :], 0.0).then_inc(made, 1)
            pool.wait_ge(k_ev, 1)
            pool.dma_start(nkp[NT * P:NT * P + 16, :], U[0:16, G:D]).then_inc(k_st, 16)
            pool.dma_start(nks, U[16:TR, G:D]).then_inc(k_st, 16)
            pool.wait_ge(v_ev, 1)
            pool.dma_start(nvp[NT * P:NT * P + 16, :], vX[0:16, :]).then_inc(v_st, 16)
            pool.dma_start(nvs, vX[16:TR, :]).then_inc(v_st, 16)
            with pool.Fori(0, NT) as it:
                pool.wait_ge(k_ev, it + 2)
                pool.dma_start(nkp[bass.ds(it * P, P), :], U[:, G:D]).then_inc(k_st, 16)
                pool.wait_ge(v_ev, it + 2)
                pool.dma_start(nvp[bass.ds(it * P, P), :],
                               V[:, bass.ds(it, 1), :].rearrange("p a n -> p (a n)")).then_inc(v_st, 16)
                pool.wait_ge(y_ready, after(it + 1, ONE_ON))
                pool.dma_start(y_att_dram[bass.ds(it, 1), :, :].rearrange("a p n -> p (a n)"), oh[:, :]).then_inc(v_st, 16)
            for n in range(4):
                if n == 0:
                    pool.wait_ge(proj, 4 * KALL)
                pool.dma_start(W[:, n], win[:, :, n * G:(n + 1) * G]).then_inc(wB, 16)
            pool.wait_ge(P_tr, after(blocks_before(4, 0) + 40, ONE_ON))
            pool.wait_ge(PV_done, after(blocks_before(4, 0) + 40, TWO_FREE))
            pool.wait_ge(v_st, 32 + 32 * NT)
            pool.dma_start(Wo, wout).then_inc(wO, 16)
            pool.dma_start(fw, final_norm_w.rearrange("(a d) -> a d", a=1).partition_broadcast(P)
                           .rearrange("p a d -> p (a d)")).then_inc(wO, 16)
            load_x(pool, hbuf, hx_load, 0)
            pool.dma_start(ycat[:, G:D], y_att_dram[0]).then_inc(ya_load, 16)
            pool.memset(masks[:, 1:8, :], 0.0).then_inc(b_made, 1)
            pool.memset(S_, 0.0).then_inc(b_made, 1)
            pool.memset(Am, 0.0).then_inc(b_made, 1)
            pool.wait_ge(b_made, 3)
            for l in range(1, 8):
                m = 1 << (l - 1)
                pool.memset(masks[:, l, :].rearrange("p (j two m) -> p j two m", two=2, m=m)[:, :, 1, :], 1.0).then_inc(b_made, 1)
            pool.wait_ge(b_made, 10)
            for l in range(1, 8):
                m = 1 << (l - 1)
                v = masks[:, l, :].rearrange("p (j two m) -> p j two m", two=2, m=m)[:, :, 1, :]
                nj = P // (2 * m)
                pool.affine_select(out=v, in_=v, compare_op=ALU.is_ge, fill=0.0, base=0,
                                   pattern=[[-2 * m, nj], [0, m]], channel_multiplier=1).then_inc(b_made, 1)
            pool.wait_ge(b_made, 17)
            for l in range(1, 8):
                m = 1 << (l - 1)
                v = masks[:, l, :].rearrange("p (j two m) -> p j two m", two=2, m=m)[:, :, 1, :]
                nj = P // (2 * m)
                pool.affine_select(out=v, in_=v, compare_op=ALU.is_ge, fill=0.0, base=m - 1,
                                   pattern=[[2 * m, nj], [0, m]], channel_multiplier=-1).then_inc(b_made, 1)
            pool.wait_ge(y_tr, 2)
            pool.dma_start(ycat[:, G:D], y_att_dram[1]).then_inc(ya_load, 16)
            pool.wait_ge(y_out, 1)
            pool.dma_start(yp[0:112, :], hbuf[16:P, :]).then_inc(yb_st, 16)
            pool.wait_ge(yb_st, 16)
            load_x(pool, hbuf, hx_load, 1)
            with pool.Fori(1, NT - 1) as t:
                pool.wait_ge(y_tr, 2 * t + 2)
                pool.dma_start(ycat[:, G:D], y_att_dram[bass.ds(t + 1, 1), :, :].rearrange("a p n -> p (a n)")).then_inc(ya_load, 16)
                pool.wait_ge(y_out, t + 1)
                pool.dma_start(yp[bass.ds(t * P - 16, 16), :], hbuf[0:16, :]).then_inc(yb_st, 16)
                pool.dma_start(yp[bass.ds(t * P, 112), :], hbuf[16:P, :]).then_inc(yb_st, 16)
                pool.wait_ge(yb_st, t * 32 + 16)
                load_x(pool, hbuf, hx_load, t + 1)
            pool.wait_ge(y_out, NT)
            t = NT - 1
            pool.dma_start(yp[t * P - 16:t * P, :], hbuf[0:16, :]).then_inc(yb_st, 16)
            pool.dma_start(yp[t * P:t * P + 112, :], hbuf[16:P, :]).then_inc(yb_st, 16)
            pool.wait_ge(yb_st, 32 * NT - 16)
            load_tail(pool, hbuf, hx_load)

        @block.scalar
        def _(act):
            for n in range(4):
                act.dma_start(W[:, n], win[:, :, 4 * G + n * G:4 * G + (n + 1) * G]).then_inc(wA, 16)
            xT_flat = xT[:, :, :].rearrange("p c t -> p (c t)")

            def square_x(n):
                act.wait_ge(x_loaded, 32 * (n + 1))
                need(act, proj, 4 * n)
                act.activation(xT_flat, xbuf[:, :], ACT.Square, accum_out=ssx[:, 0:1]).then_inc(ss_ready, 1)

            def xT_out(n):
                for a in range(2):
                    act.wait_ge(x_tr, 2 * n + a + 1)
                    act.activation(xT[:, 4 * a:4 * a + 4, :].rearrange("p c t -> p (c t)"), PT[:, a, :],
                                   ACT.Copy).then_inc(xT_ready, 1)

            def stage_p(it, g):
                if g == 0:
                    return
                act.wait_ge(d_exp, g)
                need(act, v_used, after(8 * (it - 4), TWO_FREE))
                act.activation(pst[:, :], sc[:, (g - 1) % 2, bass.ds((it - 4 * g) * 16, 16), :]
                               .rearrange("p a c -> p (a c)"), ACT.Copy).then_inc(pst_ready, 1)

            def exp_blocks(i, it8, base, nb, tail=False):
                act.wait_ge(m_ready, it8 + i + 1)
                for j in range(nb):
                    need(act, P_tr, after(base + ((i - 1) * nb + j + 1 if i else 0), ONE_ON))
                    if tail and j == 4:
                        src, dst = PD[:, 0:16], P4[:, :]
                    else:
                        src, dst = PS[:, j, :], Pb[:, j, :]
                    act.activation(dst, src, ACT.Exp, bias=negm[:, i % 2, 0:1],
                                   accum_out=sums[:, i % 2, j:j + 1]).then_inc(P_ready, 1)

            def evac_blocks(i, base, nb, tail=False):
                for j in range(nb):
                    n = i * nb + j
                    act.wait_ge(P_tr, after(base + (n + 1), ONE_ON))
                    need(act, PV_done, after(base + (n - 1), TWO_FREE))
                    if tail and j == 4:
                        act.activation(PTs[0:16, n % 2, 0:P], PT[0:16, n % 2, 0:P], ACT.Copy).then_inc(PT_ev, 1)
                    else:
                        act.activation(PTs[:, n % 2, :], PT[:, n % 2, :], ACT.Copy).then_inc(PT_ev, 1)

            def d_section(k):
                if 1 <= k <= NS:
                    act.wait_ge(d_sub, k)
                    v = sc[:, (k - 1) % 2, :, :].rearrange("p a c -> p (a c)")
                    act.activation(v, v, ACT.Exp).then_inc(d_exp, 1)

            square_x(0)
            act.wait_ge(cst, 1)
            act.activation(lamw[:, 2:4], lamw[:, 0:2], ACT.Exp).then_inc(lam_e, 1)
            act.activation(lbw[:, 1, :], lbw[:, 0, :], ACT.Exp).then_inc(lam_e, 1)
            xT_out(0)
            act.wait_ge(proj, 2)
            act.activation(qX[0:TR, :], PS[0:TR, 0, :], ACT.Copy, scale=0.125).then_inc(q_ev, 1)
            act.wait_ge(proj, 3)
            act.activation(gwX[0:TR, :], PS[0:TR, 3, :], ACT.Tanh, scale=0.5).then_inc(th_ev, 1)
            act.wait_ge(proj, 4)
            act.activation(vX[0:TR, :], PS[0:TR, 2, :], ACT.Copy).then_inc(v_ev, 1)
            square_x(1)
            xT_out(1)

            def a_tile(it, g, r):
                n = it + 1
                base = blocks_before(g, r)
                nb = g + 1
                stage_p(it, g)
                act.wait_ge(proj, 4 * n + 2)
                act.activation(U[:, 0:G], PS[:, 0, :], ACT.Copy, scale=0.125).then_inc(q_ev, 1)
                act.wait_ge(proj, 4 * n + 3)
                need(act, y_ready, after(it + 0, ONE_ON))
                act.activation(gw[:, :], PS[:, 3, :], ACT.Tanh, scale=0.5).then_inc(th_ev, 1)
                act.wait_ge(qk_tr, 2 * n + 1)
                for c in range(2):
                    rows = slice(64 * c, 64 * c + 64)
                    last = act.activation(Qz[rows, c, :, :].rearrange("p h t -> p (h t)"), PT[rows, 0, :], ACT.Copy)
                last.then_inc(qT_ev, 1)
                act.wait_ge(proj, 4 * n + 4)
                act.activation(V[:, bass.ds(it, 1), :].rearrange("p a n -> p (a n)"), PS[:, 2, :], ACT.Copy).then_inc(v_ev, 1)
                exp_blocks(0, 8 * it, base, nb)
                for i in range(1, 8):
                    evac_blocks(i - 1, base, nb)
                    exp_blocks(i, 8 * it, base, nb)
                    if i == 4:
                        square_x(n + 1)
                xT_out(n + 1)
                evac_blocks(7, base, nb)
                act.wait_ge(post, after(8 * it + 8, FOUR_FREE))
                for h in range(H):
                    last = act.activation(Pb[:, 0, h * P:(h + 1) * P], oh[:, h * P:(h + 1) * P], ACT.Square, accum_out=ssO[:, h:h + 1])
                last.then_inc(ssO_ready, 1)
                act.wait_ge(ssO_ready, it + 1)

            for g in range(4):
                d_section(g)
                with act.Fori(0, 4) as r:
                    a_tile(4 * g + r, g, r)
            base = blocks_before(4, 0)
            act.wait_ge(qX_tr, 1)
            for c in range(2):
                rows = slice(64 * c, 64 * c + 64)
                last = act.activation(Qz[rows, c, :, 0:TR], PT[rows, 0, 0:H * TR].rearrange("p (h t) -> p h t", h=H), ACT.Copy)
            last.then_inc(qT_ev, 1)
            exp_blocks(0, 8 * NT, base, 5, tail=True)
            for i in range(1, 8):
                evac_blocks(i - 1, base, 5, tail=True)
                exp_blocks(i, 8 * NT, base, 5, tail=True)
            evac_blocks(7, base, 5, tail=True)

            def yT_out(t, rows=P):
                for a in range(2):
                    act.wait_ge(y_tr, 2 * t + (a + 1))
                    act.activation(yTs[:, 4 * a:4 * a + 4, 0:rows], PT[:, a, 0:4 * rows].rearrange("p (c t) -> p c t", c=4),
                                   ACT.Copy).then_inc(yT_ev, 1)

            def square_h(t, junk, rows=P):
                act.wait_ge(h_add, after(t + 1, ONE_ON))
                act.activation(junk[0:rows, :], hbuf[0:rows, :], ACT.Square, accum_out=ssx[0:rows, 1:2]).then_inc(ssH, 1)

            def b_tile(t, g, first=False):
                it = t + NT
                n = t + KALL
                stage_p(it, g)
                act.wait_ge(proj, 4 * n + 2)
                act.activation(U[:, 0:G], PS[:, 0, :], ACT.Copy).then_inc(q_ev, 1)
                act.wait_ge(proj, 4 * n + 3)
                act.wait_ge(y_ready, after(NT, ONE_ON))
                need(act, yB, after(t + 0, ONE_ON))
                act.activation(gw[:, :], PS[:, 3, :], ACT.Tanh, scale=0.5).then_inc(th_ev, 1)
                act.wait_ge(qk_tr, 2 * n + 1)
                need(act, x_lev, after(8 * t, ONE_ON))
                need(act, s_upd, after(t + 0, ONE_ON))
                act.activation(qT, PT[:, 0, :], ACT.Copy).then_inc(qT_ev, 1)
                act.wait_ge(qk_tr, 2 * n + 2)
                act.activation(PP, PT[:, 1, :], ACT.Tanh, scale=0.5).then_inc(z_ev, 1)
                act.wait_ge(proj, 4 * n + 4)
                act.activation(ib, PS[:, 2, :], ACT.Copy).then_inc(v_ev, 1)
                square_x(n + 1)
                if not first:
                    yT_out(t - 1)
                xT_out(n + 1)
                if not first:
                    square_h(t - 1, oh_wide)
                act.wait_ge(kd_tr, t + 1)
                act.activation(kd, PT[:, 0, :], ACT.Copy).then_inc(kd_ev, 1)
                act.wait_ge(o_done, t + 1)
                for h in range(H):
                    last = act.activation(oh[:, h * P:(h + 1) * P], PO[:, h * P:(h + 1) * P], ACT.Square, accum_out=ssO[:, h:h + 1])
                last.then_inc(ssR, 1)

            oh_wide = PTs[:, :, :].rearrange("p a n -> p (a n)")
            for g in range(4, 8):
                d_section(g)
                if g == 4:
                    b_tile(0, g, first=True)
                with act.Fori(1 if g == 4 else 0, 4) as r:
                    b_tile(4 * (g - 4) + r, g)
            d_section(8)
            n = 2 * KALL - 1
            stage_p(2 * NT, 8)
            act.wait_ge(proj, 4 * n + 2)
            act.activation(U[0:TR, 0:G], PS[0:TR, 0, :], ACT.Copy).then_inc(q_ev, 1)
            act.wait_ge(proj, 4 * n + 3)
            act.wait_ge(yB, after(NT, ONE_ON))
            act.wait_ge(x_lev, after(8 * NT, ONE_ON))
            act.wait_ge(s_upd, after(NT, ONE_ON))
            act.activation(gw[0:TR, :], PS[0:TR, 3, :], ACT.Tanh, scale=0.5).then_inc(th_ev, 1)
            act.wait_ge(qk_tr, 2 * n + 1)
            act.activation(qT[:, 0:H * TR], PT[:, 0, 0:H * TR], ACT.Copy).then_inc(qT_ev, 1)
            act.wait_ge(qk_tr, 2 * n + 2)
            act.activation(PP[:, 0:H * TR], PT[:, 1, 0:H * TR], ACT.Tanh, scale=0.5).then_inc(z_ev, 1)
            act.wait_ge(proj, 4 * n + 4)
            act.activation(ib[0:TR, :], PS[0:TR, 2, :], ACT.Copy).then_inc(v_ev, 1)
            yT_out(NT - 1)
            stage_p(2 * NT + 1, 8)
            square_h(NT - 1, xT_flat)
            act.wait_ge(t_pe, 1)
            act.activation(kd[0:16, :], PT[0:16, 0, :], ACT.Copy).then_inc(t_act, 1)
            act.activation(kX[0:TR, :], PT[0:TR, 1, :], ACT.Copy).then_inc(t_act, 1)
            stage_p(2 * NT + 2, 8)
            act.wait_ge(o_done, NT + 1)
            for h in range(H):
                last = act.activation(oh[0:TR, h * P:(h + 1) * P], PO[0:TR, h * P:(h + 1) * P], ACT.Square,
                                      accum_out=ssO[0:TR, h:h + 1])
            last.then_inc(ssR, 1)
            stage_p(2 * NT + 3, 8)
            act.wait_ge(t_dve, 5)
            for h in range(H):
                last = act.activation(oh[0:TR, h * P:(h + 1) * P], oX[0:TR, h * P:(h + 1) * P], ACT.Square,
                                      accum_out=ssO[0:TR, h:h + 1])
            last.then_inc(ssR, 1)
            yT_out(NT, TR)
            square_h(NT, xT_flat, TR)

        @block.vector
        def _(ve):
            link = Chain(ve, dve)

            def rsqrt(dst, ss, inv_n):
                w = ss.shape[-1]
                rows = ss.shape[0]
                y, xh, t = dst, rsb[0:rows, 1, 0:w], rsb[0:rows, 2, 0:w]
                link(ve.tensor_scalar(xh, ss, inv_n, EPS, ALU.mult, ALU.add))
                link(ve.tensor_scalar(y.bitcast(I32), xh.bitcast(I32), -0.5, RSQRT_SEED, ALU.mult, ALU.add))
                for _ in range(3):
                    link(ve.scalar_tensor_tensor(out=t, in0=y, scalar=-0.5, in1=y, op0=ALU.mult, op1=ALU.mult))
                    link(ve.tensor_tensor(t, t, xh, ALU.mult))
                    link(ve.scalar_tensor_tensor(out=y, in0=t, scalar=1.5, in1=y, op0=ALU.add, op1=ALU.mult))

            rs = rsb[:, 0, :]

            def norm_x(n):
                ve.wait_ge(ss_ready, n + 1)
                rsqrt(rs[:, 0:1], ssx[:, 0:1], 1.0 / D)
                need(ve, qk_tr, 2 * n)
                ve.scalar_tensor_tensor(out=U[:, :], in0=xbuf[:, :], scalar=rs[:, 0:1], in1=normw[:, :],
                                        op0=ALU.mult, op1=ALU.mult).then_inc(xn_ready, 1)

            def gate(n, dst, w4, rows=P):
                ve.wait_ge(th_ev, n + 1)
                link(ve.scalar_tensor_tensor(out=dst, in0=dst, scalar=1.0, in1=PS[0:rows, 3, :], op0=ALU.add, op1=ALU.mult))
                d3 = dst.rearrange("p (h d) -> p h d", h=H)
                ve.tensor_tensor(d3, d3, w4[0:rows, :].unsqueeze(1).to_broadcast([rows, H, P]), ALU.mult).then_inc(g_ev, 1)

            def key_slot(it, s, g):
                ve.wait_ge(k_load[s % 2], (it * 4 + (s // 2 + 1)) * 32)
                kp = Kt[:, s % 2]
                link(ve.tensor_tensor(kp, kp, qb[:, :].unsqueeze(1).to_broadcast([P, 2, G]), ALU.mult))
                r16 = (it - 4 * g) * 16 + 2 * s
                ve.tensor_reduce(sc[:, g % 2, bass.ds(r16, 2), :].rearrange("p a c -> p (a c)"),
                                 kp.rearrange("p a (c d) -> p (a c) d", d=64), X, ALU.add).then_inc(k_used, 1)

            def d_section(k, close=True, open_=True):
                link.flat()
                if k >= 2 and close:
                    ve.wait_ge(d_v1, k - 1)
                    need(ve, d_qb, min(k, NS))
                    for h in range(H):
                        last = ve.tensor_scalar(tmpD[:, h * P:(h + 1) * P], PD[:, h * P:(h + 1) * P],
                                                coefD[:, k % 2:k % 2 + 1], hmask[:, h:h + 1], ALU.mult, ALU.mult)
                    last.then_inc(d_om, 1)
                    ve.wait_ge(d_cmb, k - 1)
                    ve.tensor_tensor(oX[0:TR, :], oX[0:TR, :], PS[0:TR, 0, :], ALU.add).then_inc(d_row, 1)
                    ve.wait_ge(d_row, k - 1)
                if 1 <= k <= NS and open_:
                    s = sc[:, (k - 1) % 2]
                    ve.wait_ge(k_used, after(32 * k, TWO_FREE))
                    link(ve.memset(s[:, NPG, :], -BIG))
                    link(ve.tensor_scalar(s[0:32, NPG, :], sNew[0:32, :], selm[0:32, k - 1:k], None, ALU.add))
                    ve.tensor_reduce(mpart[:, :], s.rearrange("p a c -> p c a"), X, ALU.max).then_inc(d_mx, 1)
                    ve.wait_ge(d_mxT, k)
                    link(ve.tensor_reduce(mx8[:, :], PS[0:HC, 1, 0:P], X, ALU.max))
                    ve.tensor_scalar(mxd[:, :], ident[0:HC, 0:HC], mx8[:, 0:1], None, ALU.mult).then_inc(d_mxd, 1)
                    ve.wait_ge(d_mb, k)
                    ve.tensor_tensor(s, s, PS[:, 2, 0:HC].unsqueeze(1).to_broadcast([P, NPG + 1, HC]),
                                     ALU.subtract).then_inc(d_sub, 1)
                    ve.wait_ge(d_exp, k)
                    link(ve.tensor_reduce(psums[:, :], s.rearrange("p a c -> p c a"), X, ALU.add))
                    ve.tensor_copy(srep[:, :].rearrange("p (j c) -> p j c", j=4)[:, :, 0:HC],
                                   psums[:, :].unsqueeze(1).to_broadcast([P, 4, HC])).then_inc(d_sr, 1)
                    ve.wait_ge(d_L, k)
                    c = coefD[:, (k - 1) % 2:(k - 1) % 2 + 1]
                    link(ve.reciprocal(c, PS[:, 3, 0:1]))
                    link(ve.tensor_tensor(c, c, sgn[:, :], ALU.mult))
                if k < NS and open_:
                    if k >= 2:
                        need(ve, pst_ready, 4 * (k - 1))
                        need(ve, d_cmb, k - 1)
                    ve.tensor_scalar(tmpD[0:TR, :], qX[0:TR, :], ident[0:TR, 16 + k:17 + k], None, ALU.mult).then_inc(d_qm, 1)
                    ve.wait_ge(d_qb, k + 1)
                    ve.tensor_copy(qb[:, :], PS[:, 0, :]).then_inc(d_end, 1)
                    ve.wait_ge(d_end, k + 1)
                elif k == NS:
                    ve.nop().then_inc(d_end, 1)
                link.flat()

            ve.wait_ge(const_in, 16 * 8)
            ve.wait_ge(made, 12)
            for n in range(2):
                link(ve.tensor_tensor(lamr[:, 2 * n, :], lamr[:, 2 * n, :], lamr[:, 2 * n + 1, :], ALU.mult))
                link(ve.tensor_reduce(lamw[:, n:n + 1], lamr[:, 2 * n, :], X, ALU.add))
            ve.tensor_tensor(lbw[:, 0, :], lbl[:, :], lbl[:, :], ALU.subtract).then_inc(cst, 1)
            link(ve.tensor_copy(identb[:, :], ident[:, :]))
            link(ve.tensor_reduce(hmask[:, :], ident[:, :].rearrange("p (j x h c) -> p h x j c", j=4, x=4, c=2)[:, :, 0], XY, ALU.add))
            link(ve.tensor_reduce(sgn[:, :], ident[:, 1:P:2], X, ALU.add))
            link(ve.tensor_scalar(selm[:, :], ident[:, 16:16 + NS], -1.0, BIG, ALU.add, ALU.mult))
            link(ve.tensor_scalar(subw[:, :], subw[:, :], 0.5 * (1.0 - LAM0), None, ALU.mult))
            link(ve.tensor_scalar(hgw[:, :], hgw[:, :], 0.5, None, ALU.mult))
            link(ve.memset(sNew[:, :], 0.0))
            link(ve.memset(oX[:, :], 0.0))
            link(ve.memset(PD[:, :], 0.0))
            for n, (s, v) in enumerate(((k_used, TWO_FREE), (v_used, TWO_FREE), (PT_ev, TWO_FREE), (PV_done, TWO_FREE),
                                        (post, FOUR_FREE), (P_tr, ONE_ON), (y_ready, ONE_ON), (x_lev, ONE_ON),
                                        (s_upd, ONE_ON), (yB, ONE_ON), (yT_ev, ONE_ON), (h_add, ONE_ON),
                                        (P_ready, ONE_ON), (a_cp, ONE_ON))):
                ve.memset(start[:, n:n + 1], 0.0).then_inc(s, v)
            ve.wait_ge(lam_e, 2)
            link(ve.tensor_tensor(nlam[:, :], lamw[:, 3:4], lamw[:, 2:3], ALU.subtract))
            link(ve.tensor_scalar(nlam[:, :], nlam[:, :], -LAM0, None, ALU.add))
            link(ve.tensor_scalar(lamw[:, 4:5], nlam[:, :], -1.0, None, ALU.add))
            link(ve.tensor_tensor(lamw[:, 5:6], sgn[:, :], lamw[:, 4:5], ALU.mult))
            link(ve.tensor_scalar(sgn[:, :], lamw[:, 5:6], 1.0, None, ALU.add))
            link(ve.reciprocal(lbw[:, 2, :], lbw[:, 1, :]))
            link(ve.tensor_tensor(lbw[:, 3, :], lbw[:, 1, :], lbw[:, 2, :], ALU.mult))
            link(ve.tensor_tensor(lbw[:, 0, :], lbw[:, 3, :], lbw[:, 3, :], ALU.subtract))
            link(ve.tensor_scalar(lbw[:, 1, :], lbw[:, 0, :], -0.5, 0.5, ALU.mult, ALU.add))
            link(ve.tensor_scalar(lbw[:, 2, :], lbw[:, 1, :], -1.0, None, ALU.mult))
            link(ve.tensor_tensor(lbw[:, 3, :], lbw[:, 0, :], lbw[:, 1, :], ALU.add))
            ve.tensor_copy(mx8[:, :], ones[0:HC, 0:1]).then_inc(cst2, 1)
            norm_x(0)
            ve.wait_ge(proj, 1)
            ve.tensor_copy(U[0:TR, G:D], PS[0:TR, 1, :]).then_inc(k_ev, 1)
            gate(0, gwX[0:TR, :], subw, TR)
            ve.wait_ge(qk_tr, 2)
            ve.tensor_copy(KT[:, :, NT * P:NT * P + 16], PT[:, 1, 0:H * TR].rearrange("p (h t) -> p h t", h=H)[:, :, 0:16])\
                .then_inc(kT_ev, 1)
            ve.wait_ge(q_ev, 1)
            ve.wait_ge(k_ev, 1)
            link(ve.tensor_tensor(tmpD[0:TR, :], qX[0:TR, :], U[0:TR, G:D], ALU.mult))
            link(ve.tensor_reduce(sNew[0:TR, :], tmpD[0:TR, :].rearrange("p (c d) -> p c d", d=64), X, ALU.add))
            ve.wait_ge(k_st, 32)
            norm_x(1)
            link.flat()

            def post_block(i, it, base, nb, first):
                ve.wait_ge(PV_done, after(base + (i + 1) * nb, TWO_FREE))
                h, c = i // 2, i % 2
                if nb > 1:
                    link(ve.tensor_reduce(rcp[:, 1:2], sums[:, i % 2, 0:nb], X, ALU.add))
                    link(ve.reciprocal(rcp[:, 0:1], rcp[:, 1:2]))
                else:
                    link(ve.reciprocal(rcp[:, 0:1], sums[:, i % 2, 0:1]))
                o = PO[:, (i % OUT_SLOTS) * P:(i % OUT_SLOTS + 1) * P]
                if i == 0:
                    ve.wait_ge(v_st, first)
                if c == 0:
                    ve.tensor_scalar(oh[:, h * P:(h + 1) * P], o, rcp[:, 0:1], None, ALU.mult).then_inc(post, 1)
                else:
                    link(ve.tensor_tensor(rcp[:, 0:1], rcp[:, 0:1], nlam[:, :], ALU.mult))
                    need(ve, post, after(8 * it + i, FOUR_FREE))
                    ve.scalar_tensor_tensor(out=oh[:, h * P:(h + 1) * P], in0=o, scalar=rcp[:, 0:1],
                                            in1=oh[:, h * P:(h + 1) * P], op0=ALU.mult, op1=ALU.add).then_inc(post, 1)

            def row_max(i, it, nb, tail=False):
                ve.wait_ge(S_done, it * 8 + i + 1)
                dst = negm[:, i % 2, 0:1]
                if not tail:
                    ve.tensor_reduce(dst, PS[:, 0:nb, :], XY, ALU.max, negate=True).then_inc(m_ready, 1)
                else:
                    link(ve.tensor_reduce(dst, PS[:, :, :], XY, ALU.max, negate=True))
                    link(ve.tensor_reduce(negm[:, i % 2, 1:2], PD[:, 0:16], X, ALU.max, negate=True))
                    ve.tensor_tensor(dst, dst, negm[:, i % 2, 1:2], ALU.min).then_inc(m_ready, 1)

            def head_norm(out, src, src_ready, value, gates, r4, after, rows=P, inc=True):
                ve.wait_ge(src_ready, value)
                rsqrt(r4, ssO[0:rows, :], 1.0 / P)
                for h in range(H):
                    last = ve.scalar_tensor_tensor(out=out[:, h * P:(h + 1) * P], in0=src[:, h * P:(h + 1) * P],
                                                   scalar=r4[:, h:h + 1], in1=gates[:, h * P:(h + 1) * P],
                                                   op0=ALU.mult, op1=ALU.mult)
                last.then_inc(after, 1)

            for g in range(4):
                d_section(g)
                nb = g + 1
                steps = 1 + SLOTS + 8 * (2 if nb > 1 else 1) + 4 + 2 * RS_STEPS
                link.enter(0, steps)
                with ve.Fori(0, 4) as r:
                    link.r = r
                    it = 4 * g + r
                    n = it + 1
                    base = blocks_before(g, r)
                    key_slot(it, 0, g)
                    key_slot(it, 1, g)
                    ve.wait_ge(proj, 4 * n + 1)
                    ve.tensor_copy(U[:, G:D], PS[:, 1, :]).then_inc(k_ev, 1)
                    key_slot(it, 2, g)
                    gate(n, gw[:, :], subw)
                    ve.wait_ge(qk_tr, 2 * n + 2)
                    ve.tensor_copy(KT[:, :, bass.ds(it * P, P)], PT[:, 1, :].rearrange("p (h t) -> p h t", h=H))\
                        .then_inc(kT_ev, 1)
                    key_slot(it, 3, g)
                    for i in range(8):
                        row_max(i, it, nb)
                        if i % 2:
                            key_slot(it, 4 + i // 2, g)
                        if i >= 1:
                            post_block(i - 1, it, base, nb, 32 * it + 48)
                        if i == 5:
                            ve.wait_ge(k_st, 32 + 16 * (it + 1))
                            norm_x(n + 1)
                    post_block(7, it, base, nb, 32 * it + 48)
                    head_norm(oh, oh, ssO_ready, it + 1, gw, rs, y_ready)
                link.leave(4)
            base = blocks_before(4, 0)
            d_section(4, open_=False)
            for i in range(8):
                row_max(i, NT, 5, tail=True)
                if i >= 1:
                    post_block(i - 1, NT, base, 5, 32 * NT + 32)
            post_block(7, NT, base, 5, 32 * NT + 32)
            ve.wait_ge(post, after(8 * NT + 8, FOUR_FREE))
            link(ve.tensor_copy(oX[0:16, :], oh[0:16, :]))
            ve.wait_ge(PV_done, after(base + 40, TWO_FREE))
            ve.wait_ge(made, 12)
            ve.tensor_copy(masks[:, 0, :], ident[:, :]).then_inc(b_init, 1)
            ve.wait_ge(b_made, 24)
            ve.wait_ge(b_init, 1)
            link.flat()

            def forget(cols):
                for h in range(H):
                    a = slice(h * cols, (h + 1) * cols)
                    last = ve.tensor_scalar(kT[:, a], PP[:, a], lbw[:, 2, h:h + 1], lbw[:, 1, h:h + 1], ALU.mult, ALU.add)
                link(last)
                for h in range(H):
                    a = slice(h * cols, (h + 1) * cols)
                    last = ve.tensor_scalar(PP[:, a], PP[:, a], lbw[:, 1, h:h + 1], lbw[:, 3, h:h + 1], ALU.mult, ALU.add)
                last.then_inc(kf, 1)

            def halves(ap, m):
                return ap.rearrange("p (j two m) -> p j two m", two=2, m=m)

            def add_residual(t, rows=P):
                ve.wait_ge(h_mm, t + 1)
                ve.wait_ge(hx_load, 32 * (t + 1))
                hv = hbuf[0:rows, :].rearrange("p (a n) -> p a n", a=2)
                ve.tensor_tensor(hv, hv, PS[0:rows, 0:2, :], ALU.add).then_inc(h_add, 1)

            def final_norm(t, rows=P):
                ve.wait_ge(ssH, t + 1)
                rsqrt(rs[0:rows, 0:1], ssx[0:rows, 1:2], 1.0 / D)
                ve.scalar_tensor_tensor(out=hbuf[0:rows, :], in0=hbuf[0:rows, :], scalar=rs[0:rows, 0:1], in1=fw[0:rows, :],
                                        op0=ALU.mult, op1=ALU.mult).then_inc(y_out, 1)

            def b_tile(t, g, first=False):
                it = t + NT
                n = t + KALL
                key_slot(it, 0, g)
                if not first:
                    head_norm(ycat[:, 0:G], PO[:, :], ssR, t, gw, rs, yB)
                key_slot(it, 1, g)
                ve.wait_ge(proj, 4 * n + 1)
                ve.tensor_copy(U[:, G:D], PS[:, 1, :]).then_inc(k_ev, 1)
                key_slot(it, 2, g)
                link(ve.memset(QQ, 1.0))
                key_slot(it, 3, g)
                gate(n, gw[:, :], hgw)
                ve.wait_ge(z_ev, t + 1)
                forget(P)
                key_slot(it, 4, g)
                key_slot(it, 5, g)
                ve.wait_ge(kf, t + 1)
                ve.wait_ge(qT_ev, n)
                for l in range(8):
                    if l >= 1:
                        m = 1 << (l - 1)
                        xl, q, k, p_, q_ = (halves(a, m) for a in (Xl[l % 2], qT, kT, PP, QQ))
                        if l >= 3:
                            ve.wait_ge(a_lev, 8 * t + (l - 1))
                        ve.tensor_tensor(xl[:, :, 1, :], q[:, :, 1, :], p_[:, :, 1, :], ALU.mult)
                        ve.tensor_tensor(xl[:, :, 0, :], k[:, :, 0, :], q_[:, :, 0, :], ALU.mult).then_inc(x_lev, 1)
                        shape = [P, 4 * P // (2 * m), m]
                        link(ve.tensor_tensor(q_[:, :, 0, :], q_[:, :, 0, :], p_[:, :, 1, m - 1:m].to_broadcast(shape), ALU.mult))
                        link(ve.tensor_tensor(p_[:, :, 1, :], p_[:, :, 1, :], p_[:, :, 0, m - 1:m].to_broadcast(shape), ALU.mult))
                        predicated(ve, l - 1, t, a_lev, a_cp, Am, masks, PS, mpart)
                    if l in (1, 6):
                        key_slot(it, 6 if l == 1 else 7, g)
                    if l == 3:
                        norm_x(n + 1)
                ve.tensor_tensor(XQ, qT, PP, ALU.mult)
                ve.tensor_tensor(XK, kT, QQ, ALU.mult).then_inc(x_lev, 1)
                predicated(ve, 7, t, a_lev, a_cp, Am, masks, PS, mpart)
                if not first:
                    add_residual(t - 1)
                ve.wait_ge(su, t + 1)
                ve.wait_ge(o_done, t + 1)
                for h in range(H):
                    a = slice(h * P, (h + 1) * P)
                    last = ve.scalar_tensor_tensor(out=S_[:, a], in0=S_[:, a], scalar=PP[:, h * P + P - 1:h * P + P],
                                                   in1=PS[:, SU_BANK, a], op0=ALU.mult, op1=ALU.add)
                last.then_inc(s_upd, 1)
                if not first:
                    final_norm(t - 1)

            for g in range(4, 8):
                d_section(g, close=g > 4)
                if g == 4:
                    b_tile(0, g, first=True)
                    link.flat()
                head = 1 if g == 4 else 0
                link.enter(head, 1 + SLOTS + 2 + 2 * 7 + 3 * RS_STEPS)
                with ve.Fori(head, 4) as r:
                    link.r = r
                    b_tile(4 * (g - 4) + r, g)
                link.leave(4 - head)
            d_section(8)
            n = 2 * KALL - 1
            head_norm(ycat[:, 0:G], PO[:, :], ssR, NT, gw, rs, yB)
            ve.wait_ge(proj, 4 * n + 1)
            ve.tensor_copy(U[0:TR, G:D], PS[0:TR, 1, :]).then_inc(k_ev, 1)
            gate(n, gw[0:TR, :], hgw, TR)
            ve.wait_ge(ssH, NT - 1)
            link(ve.memset(QQ, 1.0))
            link(ve.memset(PTs[:, 0, :], 0.0))
            link(ve.memset(QM, 0.0))
            ve.wait_ge(z_ev, NT + 1)
            forget(TR)
            ve.wait_ge(kf, NT + 1)
            ve.wait_ge(qT_ev, n)
            q3, k3, p3, qq3 = (a[:, 0:H * TR].rearrange("p (h t) -> p h t", h=H) for a in (qT, kT, PP, QQ))
            x3 = [a[:, 0:H * TR].rearrange("p (h t) -> p h t", h=H) for a in Xl]
            link(ve.tensor_copy(fX, p3))
            for h in range(H):
                last = ve.tensor_copy(QM[:, h, 16:16 + 25 * (NS - 1) + 1:25], q3[:, h, 16:TR])
            last.then_inc(t_dve, 1)

            def sub(ap, h, m, half):
                return ap[:, h, 0:16].rearrange("p (j two m) -> p j two m", two=2, m=m)[:, :, half, :]

            for l in range(5):
                if l >= 1:
                    m = 1 << (l - 1)
                    if l >= 3:
                        ve.wait_ge(a_lev, 8 * NT + (l - 1))
                    for h in range(H):
                        ve.tensor_tensor(sub(x3[l % 2], h, m, 1), sub(q3, h, m, 1), sub(p3, h, m, 1), ALU.mult)
                        last = ve.tensor_tensor(sub(x3[l % 2], h, m, 0), sub(k3, h, m, 0), sub(qq3, h, m, 0), ALU.mult)
                    last.then_inc(x_lev, 1)
                    for h in range(H):
                        shape = [P, 16 // (2 * m), m]
                        link(ve.tensor_tensor(sub(qq3, h, m, 0), sub(qq3, h, m, 0), sub(p3, h, m, 1)[:, :, m - 1:m].to_broadcast(shape), ALU.mult))
                        link(ve.tensor_tensor(sub(p3, h, m, 1), sub(p3, h, m, 1), sub(p3, h, m, 0)[:, :, m - 1:m].to_broadcast(shape), ALU.mult))
                    tail_predicated(ve, l - 1, a_lev, a_cp, AX, masks, PS)
            ve.tensor_tensor(qPX[:, :, 0:16], q3[:, :, 0:16], p3[:, :, 0:16], ALU.mult)
            xk3 = XK[:, 0:H * TR].rearrange("p (h t) -> p h t", h=H)
            ve.tensor_tensor(xk3[:, :, 0:16], k3[:, :, 0:16], qq3[:, :, 0:16], ALU.mult).then_inc(x_lev, 1)
            tail_predicated(ve, 4, a_lev, a_cp, AX, masks, PS)
            add_residual(NT - 1)
            final_norm(NT - 1)
            ve.wait_ge(t_act, 2)
            ve.wait_ge(st_in, 16)
            for b in range(NS):
                need(ve, t_pe, b + 1)
                link(ve.tensor_scalar(kmX[0:TR, :], kX[0:TR, :], ident[0:TR, 16 + b:17 + b], None, ALU.mult))
                ve.nop().then_inc(bconst, 1)
                ve.wait_ge(t_pe, b + 2)
                for h in range(H):
                    sx = SX[:, b * H + h, :]
                    last = ve.scalar_tensor_tensor(out=sx, in0=sx, scalar=fX[:, h, 16 + b:17 + b],
                                                   in1=PS[:, 2 + b % 2, h * P:(h + 1) * P], op0=ALU.mult, op1=ALU.add)
                link(last)
            ve.nop().then_inc(t_dve, 1)
            ve.wait_ge(su, NT + 1)
            ve.wait_ge(o_done, NT + 1)
            for h in range(H):
                a = slice(h * P, (h + 1) * P)
                last = ve.scalar_tensor_tensor(out=S_[:, a], in0=S_[:, a], scalar=p3[:, h, 15:16],
                                               in1=PS[:, 0, a], op0=ALU.mult, op1=ALU.add)
            link(last)
            ve.nop().then_inc(t_dve, 2)
            ve.wait_ge(y_tr, 2 * NT)
            head_norm(ycat[0:TR, 0:G], PO[0:TR, :], ssR, NT + 1, gw[0:TR, :], rs[0:TR, :], yB, TR)
            d_section(9)
            ve.nop().then_inc(t_dve, 1)
            head_norm(ycat[0:TR, G:D], oX[0:TR, :], ssR, NT + 2, gwX[0:TR, :], rs[0:TR, :], yB, TR)
            add_residual(NT, TR)
            final_norm(NT, TR)

        @block.tensor
        def _(pe):
            def x_front(n, half):
                if half == 0:
                    pe.wait_ge(xn_ready, n + 1)
                for c in range(4):
                    mm = pe.transpose(PT[:, half, c * P:(c + 1) * P], U[:, (4 * half + c) * P:(4 * half + c + 1) * P], ident[:, :])
                mm.then_inc(x_tr, 1)

            def project(n, order, rows=P, loaded=None):
                for b in order:
                    if loaded is not None:
                        pe.wait_ge(loaded, 64)
                    pe.wait_ge(xT_ready, 2 * n + 2)
                    for c in range(DC):
                        mm = pe.matmul(PS[0:rows, b, :], xT[:, c, 0:rows], W[:, b, c, :], start=(c == 0), stop=(c == DC - 1))
                    mm.then_inc(proj, 1)

            def qk_transposes(n, rows=P):
                pe.wait_ge(q_ev, n + 1)
                pe.wait_ge(k_ev, n + 1)
                for a in range(2):
                    for h in range(H):
                        mm = pe.transpose(PT[:, a, h * rows:(h + 1) * rows], U[0:rows, (4 * a + h) * P:(4 * a + h + 1) * P],
                                          ident[0:rows, 0:rows])
                    mm.then_inc(qk_tr, 1)

            def scores(i, it, base, nb, g, r, tail=False):
                h, c = i // 2, i % 2
                q = Qz[:, c, h, :]
                for j in range(nb):
                    if i:
                        pe.wait_ge(P_ready, after(base + ((i - 1) * nb + j + 1), ONE_ON))
                    if tail and j == 4:
                        mm = pe.matmul(PD[:, 0:16], q, KT[:, h, NT * P:NT * P + 16], start=True, stop=False)
                        mm = pe.matmul(PD[:, 0:16], identb[:, :], causal[:, 384:400], start=False, stop=True)
                    else:
                        diag = not tail and j == nb - 1
                        mm = pe.matmul(PS[:, j, :], q, KT[:, h, j * G:(j + 1) * G], start=True, stop=not diag)
                        if diag:
                            mm = pe.matmul(PS[:, j, :], identb[:, :], causal[:, bass.ds(r * (-P) + 384, G)], start=False, stop=True)
                mm.then_inc(S_done, 1)

            def values(i, it, base, nb, tail=False):
                h = i // 2
                slot = i % OUT_SLOTS

                def turn(j):
                    n = i * nb + j
                    pe.wait_ge(P_ready, after(base + (n + 1), ONE_ON))
                    need(pe, PT_ev, after(base + (n - 1), TWO_FREE))
                    if tail and j == 4:
                        mm = pe.transpose(PT[0:16, n % 2, 0:P], P4[:, :], ident[:, :])
                    else:
                        for u in range(4):
                            mm = pe.transpose(PT[:, n % 2, u * P:(u + 1) * P], Pb[:, j, u * P:(u + 1) * P], ident[:, :])
                    mm.then_inc(P_tr, 1)

                def add(j):
                    n = i * nb + j
                    pe.wait_ge(PT_ev, after(base + (n + 1), TWO_FREE))
                    if j == 0:
                        pe.wait_ge(post, after(8 * it + i, FOUR_FREE))
                    out = PO[:, slot * P:(slot + 1) * P]
                    if tail and j == 4:
                        mm = pe.matmul(out, PTs[0:16, n % 2, 0:P], vX[0:16, h * P:(h + 1) * P], start=False, stop=True)
                    else:
                        for u in range(4):
                            mm = pe.matmul(out, PTs[:, n % 2, u * P:(u + 1) * P], V[:, 4 * j + u, h * P:(h + 1) * P],
                                           start=(j == 0 and u == 0), stop=(j == nb - 1 and u == 3))
                    mm.then_inc(PV_done, 1)

                turn(0)
                for j in range(nb):
                    if j + 1 < nb:
                        turn(j + 1)
                    add(j)

            def value_slot(it, s, g):
                if g == 0:
                    return
                if s == 0:
                    pe.wait_ge(pst_ready, it + (-3))
                pe.wait_ge(v_load[s % 2], (it * 4 + (s // 2 + 1 - 16)) * 32)
                for u in range(2):
                    j = (2 * s + u) % 4
                    mm = pe.matmul(PD[32 * j:32 * j + HC, :], pst[:, (2 * s + u) * HC:(2 * s + u + 1) * HC], Vt[:, s % 2, u, :],
                                   start=False, stop=False, skip_group_check=True)
                mm.then_inc(v_used, 1)

            def d_section(k, close=True, open_=True):
                if k >= 2 and close:
                    for j in range(4):
                        mm = pe.matmul(PD[32 * j:32 * j + HC, :], zero8[0:TR, :], vX[0:TR, :], start=False, stop=True,
                                       skip_group_check=True)
                    mm.then_inc(d_v1, 1)
                    pe.wait_ge(d_om, k - 1)
                    b = k - 2
                    pe.matmul(PS[0:TR, 0, :], pick[:, 23 - 16 - b:23 - 16 - b + TR], tmpD[:, :], start=True, stop=True).then_inc(d_cmb, 1)
                if not open_:
                    return
                if 1 <= k <= NS:
                    pe.wait_ge(d_mx, k)
                    pe.transpose(PS[0:HC, 1, 0:P], mpart[:, :], ident[:, :]).then_inc(d_mxT, 1)
                    pe.wait_ge(d_mxd, k)
                    pe.matmul(PS[:, 2, 0:HC], ones[0:HC, :], mxd[:, :], start=True, stop=True).then_inc(d_mb, 1)
                    pe.wait_ge(d_exp, k)
                    s = sc[:, (k - 1) % 2]
                    for j in range(4):
                        w = s[0:TR, NPG, :] if j == 0 else zero8[0:TR, :]
                        pe.matmul(PD[32 * j:32 * j + HC, :], w, vX[0:TR, :], start=True, stop=False, skip_group_check=True)
                    pe.wait_ge(d_sr, k)
                    pe.matmul(PS[:, 3, 0:1], srep[:, :], ones[:, 0:1], start=True, stop=True).then_inc(d_L, 1)
                if k < NS:
                    pe.wait_ge(d_qm, k + 1)
                    pe.matmul(PS[:, 0, :], ones[0:TR, :], tmpD[0:TR, :], start=True, stop=True).then_inc(d_qb, 1)

            pe.wait_ge(cst2, 1)
            x_front(0, 0)
            x_front(0, 1)
            project(0, (1, 0, 3, 2), TR, wA)
            pe.wait_ge(k_ev, 1)
            for h in range(H):
                mm = pe.transpose(PT[:, 1, h * TR:(h + 1) * TR], U[0:TR, (4 + h) * P:(5 + h) * P], ident[0:TR, 0:TR])
            mm.then_inc(qk_tr, 2)
            pe.wait_ge(q_ev, 1)
            pe.wait_ge(v_ev, 1)
            pe.wait_ge(g_ev, 1)
            pe.wait_ge(kT_ev, 1)
            x_front(1, 0)
            x_front(1, 1)

            for g in range(4):
                d_section(g)
                nb = g + 1
                with pe.Fori(0, 4) as r:
                    it = 4 * g + r
                    n = it + 1
                    base = blocks_before(g, r)
                    pe.wait_ge(d_end, g + 1)
                    need(pe, P_ready, after(base + 0, ONE_ON))
                    project(n, (1, 0, 3))
                    pe.wait_ge(PT_ev, after(base, TWO_FREE))
                    qk_transposes(n)
                    project(n, (2,))
                    pe.wait_ge(qT_ev, n)
                    pe.wait_ge(kT_ev, n + 1)
                    if nb > 2:
                        pe.wait_ge(v_ev, n + 1)
                    if nb > 3:
                        pe.wait_ge(g_ev, n + 1)
                    scores(0, it, base, nb, g, r)
                    value_slot(it, 0, g)
                    pe.wait_ge(v_ev, n + 1)
                    pe.wait_ge(g_ev, n + 1)
                    for i in range(1, 8):
                        scores(i, it, base, nb, g, r)
                        values(i - 1, it, base, nb)
                        value_slot(it, i, g)
                    pe.wait_ge(PT_ev, after(base + 7 * nb, TWO_FREE))
                    x_front(n + 1, 0)
                    x_front(n + 1, 1)
                    pe.wait_ge(xT_ready, 2 * n + 4)
                    values(7, it, base, nb)
            base = blocks_before(4, 0)
            pe.wait_ge(P_ready, after(base, ONE_ON))
            d_section(4, open_=False)
            pe.wait_ge(d_row, 3)
            pe.wait_ge(PT_ev, after(base, TWO_FREE))
            for h in range(H):
                mm = pe.transpose(PT[:, 0, h * TR:(h + 1) * TR], qX[0:TR, h * P:(h + 1) * P], ident[0:TR, 0:TR])
            mm.then_inc(qX_tr, 1)
            pe.wait_ge(qT_ev, NT + 1)
            pe.wait_ge(P_ready, after(base, ONE_ON))
            pe.wait_ge(post, after(8 * NT, FOUR_FREE))
            scores(0, NT, base, 5, 4, 0, tail=True)
            for i in range(1, 8):
                scores(i, NT, base, 5, 4, 0, tail=True)
                values(i - 1, NT, base, 5, tail=True)
            values(7, NT, base, 5, tail=True)

            pe.wait_ge(post, after(8 * NT + 8, FOUR_FREE))
            pe.wait_ge(P_ready, after(base + 40, ONE_ON))
            pe.wait_ge(PT_ev, after(base + 40, TWO_FREE))
            pe.wait_ge(wB, 64)
            def y_transposes(t, rows=P):
                pe.wait_ge(yB, after(t + 1, ONE_ON))
                for a in range(2):
                    for c in range(4):
                        mm = pe.transpose(PT[:, a, c * rows:(c + 1) * rows], ycat[0:rows, (4 * a + c) * P:(4 * a + c + 1) * P],
                                          ident[0:rows, 0:rows])
                    mm.then_inc(y_tr, 1)

            def out_quarter(t, quarter, rows=P):
                if quarter == 0:
                    pe.wait_ge(yT_ev, after(2 * t + 2, ONE_ON))
                    pe.wait_ge(wO, 32)
                b = quarter // 2
                for c in range(4 * (quarter % 2), 4 * (quarter % 2) + 4):
                    mm = pe.matmul(PS[0:rows, b, :], yTs[:, c, 0:rows], Wo[:, c, b * G:(b + 1) * G], start=(c == 0), stop=(c == DC - 1))
                if quarter == 3:
                    mm.then_inc(h_mm, 1)

            def b_tile(t, g, first=False):
                it = t + NT
                n = t + KALL
                pe.wait_ge(d_end, g + 1)
                if not first:
                    pe.wait_ge(h_add, after(t - 1, ONE_ON))
                project(n, (1,))
                value_slot(it, 0, g)
                project(n, (0,))
                value_slot(it, 1, g)
                need(pe, s_upd, after(t + 0, ONE_ON))
                project(n, (3,))
                value_slot(it, 2, g)
                qk_transposes(n)
                project(n, (2,))
                value_slot(it, 3, g)
                pe.wait_ge(g_ev, n + 1)
                pe.wait_ge(kf, t + 1)
                pe.wait_ge(qT_ev, n)
                for l in range(8):
                    if l == 1:
                        pe.wait_ge(v_ev, n + 1)
                    if l >= 2:
                        pe.wait_ge(a_cp, after(8 * t + (l - 1), ONE_ON))
                    if l >= 1:
                        pe.wait_ge(x_lev, after(8 * t + l, ONE_ON))
                    for h in range(H):
                        a = slice(h * P, (h + 1) * P)
                        lhs, rhs = (kT[:, a], qT[:, a]) if l == 0 else (Xl[l % 2][:, a], Xl[l % 2][:, a])
                        mm = pe.matmul(PS[:, 3 - l % 2, a], lhs, rhs, start=True, stop=True)
                    mm.then_inc(a_lev, 1)
                    if l == 0 and not first:
                        pe.wait_ge(ya_load, 16 * t)
                        pe.wait_ge(z_ev, t + 1)
                        y_transposes(t - 1)
                    if 1 <= l <= 4 and not first:
                        out_quarter(t - 1, l - 1)
                    if l == 5:
                        x_front(n + 1, 0)
                    if l == 6:
                        x_front(n + 1, 1)
                    if l % 2:
                        value_slot(it, 4 + l // 2, g)
                pe.wait_ge(x_lev, after(8 * t + 8, ONE_ON))
                pe.wait_ge(xT_ready, 2 * n + 3)
                for h in range(H):
                    a = slice(h * P, (h + 1) * P)
                    mm = pe.transpose(PT[:, 0, a], XK[:, a], ident[:, :])
                mm.then_inc(kd_tr, 1)
                pe.wait_ge(a_cp, after(8 * t + 8, ONE_ON))
                need(pe, s_upd, after(t + 0, ONE_ON))
                need(pe, yB, after(t + 0, ONE_ON))
                for h in range(H):
                    a = slice(h * P, (h + 1) * P)
                    pe.matmul(PO[:, a], Am[:, a], ib[:, a], start=True, stop=False)
                    mm = pe.matmul(PO[:, a], XQ[:, a], S_[:, a], start=False, stop=True)
                mm.then_inc(o_done, 1)
                pe.wait_ge(kd_ev, t + 1)
                for h in range(H):
                    a = slice(h * P, (h + 1) * P)
                    mm = pe.matmul(PS[:, SU_BANK, a], kd[:, a], ib[:, a], start=True, stop=True)
                mm.then_inc(su, 1)

            for g in range(4, 8):
                d_section(g, close=g > 4)
                if g == 4:
                    b_tile(0, g, first=True)
                with pe.Fori(1 if g == 4 else 0, 4) as r:
                    b_tile(4 * (g - 4) + r, g)
            d_section(8)
            n = 2 * KALL - 1
            pe.wait_ge(d_end, 9)
            pe.wait_ge(s_upd, after(NT, ONE_ON))
            pe.wait_ge(h_add, after(NT - 1, ONE_ON))
            project(n, (1, 0, 3), TR)
            qk_transposes(n, TR)
            project(n, (2,), TR)
            pe.wait_ge(v_ev, n + 1)
            pe.wait_ge(g_ev, n + 1)
            pe.wait_ge(kf, NT + 1)
            pe.wait_ge(qT_ev, n)
            for l in range(5):
                if l >= 2:
                    pe.wait_ge(a_cp, after(8 * NT + (l - 1), ONE_ON))
                if l >= 1:
                    pe.wait_ge(x_lev, after(8 * NT + l, ONE_ON))
                for h in range(H):
                    a = slice(h * TR, h * TR + 16)
                    lhs, rhs = (kT[:, a], qT[:, a]) if l == 0 else (Xl[l % 2][:, a], Xl[l % 2][:, a])
                    mm = pe.matmul(PS[0:16, 3 - l % 2, h * 16:(h + 1) * 16], lhs, rhs, start=True, stop=True)
                mm.then_inc(a_lev, 1)
                if l == 0:
                    pe.wait_ge(ya_load, 16 * NT)
                    pe.wait_ge(z_ev, NT + 1)
                    y_transposes(NT - 1)
                else:
                    out_quarter(NT - 1, l - 1)
                    value_slot(2 * NT, 2 * l - 2, 8)
                    value_slot(2 * NT, 2 * l - 1, 8)
            pe.wait_ge(x_lev, after(8 * NT + 5, ONE_ON))
            for h in range(H):
                pe.transpose(PT[0:16, 0, h * P:(h + 1) * P], XK[:, h * TR:h * TR + 16], ident[:, :])
            for h in range(H):
                mm = pe.transpose(PT[0:TR, 1, h * P:(h + 1) * P], kT[:, h * TR:(h + 1) * TR], ident[:, :])
            mm.then_inc(t_pe, 1)
            for b in range(NS):
                pe.wait_ge(bconst, b + 1)
                if b == 0:
                    pe.wait_ge(a_cp, after(8 * NT + 5, ONE_ON))
                for h in range(H):
                    a = slice(h * P, (h + 1) * P)
                    mm = pe.matmul(PS[:, 2 + b % 2, a], kmX[0:TR, a], ib[0:TR, a], start=True, stop=True)
                mm.then_inc(t_pe, 1)
                value_slot(2 * NT + 1, b, 8)
            pe.wait_ge(t_act, 2)
            pe.wait_ge(h_add, after(NT, ONE_ON))
            for h in range(H):
                a = slice(h * P, (h + 1) * P)
                mm = pe.matmul(PS[:, 0, a], kd[0:16, a], ib[0:16, a], start=True, stop=True)
            mm.then_inc(su, 1)
            pe.wait_ge(t_dve, 2)
            pe.wait_ge(yB, after(NT, ONE_ON))
            for h in range(H):
                a = slice(h * P, (h + 1) * P)
                pe.matmul(PO[0:TR, a], AX[0:16, h, :], ib[0:16, a], start=True, stop=False)
                pe.matmul(PO[0:TR, a], qPX[:, h, :], S_[:, a], start=False, stop=False)
                for b in range(NS):
                    mm = pe.matmul(PO[0:TR, a], QM[:, h, b * TR:(b + 1) * TR], SX[:, b * H + h, :], start=False, stop=(b == NS - 1))
            mm.then_inc(o_done, 1)
            with pe.Fori(2 * NT + 2, 2 * NT + 4) as it:
                for s in range(SLOTS):
                    value_slot(it, s, 8)
            d_section(9)
            pe.wait_ge(yB, after(NT + 2, ONE_ON))
            y_transposes(NT, TR)
            for quarter in range(4):
                out_quarter(NT, quarter, TR)


def predicated(ve, l, t, a_lev, a_cp, Am, masks, PS, spare):
    ve.wait_ge(a_lev, 8 * t + (l + 1))
    need(ve, a_cp, after(8 * t + l, ONE_ON))
    ve.tensor_copy(spare[:, l:l + 1], masks[:, 0, 0:1])
    ve.copy_predicated(Am.rearrange("p (h t) -> p h t", h=H),
                       masks[:, l, :].bitcast(U32).unsqueeze(1).to_broadcast([P, H, P]),
                       PS[:, 3 - l % 2, :].rearrange("p (h t) -> p h t", h=H)).then_inc(a_cp, 1)


def tail_predicated(ve, l, a_lev, a_cp, AX, masks, PS):
    ve.wait_ge(a_lev, 8 * NT + (l + 1))
    ve.wait_ge(a_cp, after(8 * NT + l, ONE_ON))
    ve.copy_predicated(AX[0:16, :, 0:16], masks[0:16, l, 0:16].bitcast(U32).unsqueeze(1).to_broadcast([16, H, 16]),
                       PS[0:16, 3 - l % 2, 0:64].rearrange("p (h t) -> p h t", h=H)).then_inc(a_cp, 1)


_INS = ['x_prompt', 'x_sample', 'cache_k', 'cache_v', 'state_hgrn', 'page_table', 'meta_tokens', 'norm_w', 'w_in',
        'w_out', 'lb_logits', 'hgrn_norm_w', 'subln_w', 'lam_q1', 'lam_k1', 'lam_q2', 'lam_k2', 'final_norm_w']
_OUTS = [((1, 2048, 1024), 'float32'), ((8, 1, 1024), 'float32'), ((1, 1, 2064, 4, 128), 'float32'),
         ((1, 1, 2064, 4, 128), 'float32'), ((1, 1, 4, 128, 128), 'float32'), ((1, 8, 1, 4, 128), 'float32'),
         ((1, 8, 1, 4, 128), 'float32'), ((1, 8, 4, 128, 128), 'float32')]


def kernel(**inputs):
    import numpy as _np
    import concourse.bacc as _bacc
    from concourse import mybir as _mybir
    from concourse.bass_utils import run_bass_kernel_spmd as _run

    nc = _bacc.Bacc("TRN2", target_bir_lowering=False, num_devices=1)
    arrays, args = {}, []
    for name in _INS:
        a = _np.ascontiguousarray(inputs[name])
        arrays[f"in_{name}_dram"] = a
        args.append(nc.dram_tensor(f"in_{name}_dram", a.shape, _mybir.dt.from_np(a.dtype), kind="ExternalInput").ap())
    for i, (shape, dtype) in enumerate(_OUTS):
        dt = _mybir.dt.from_np(_np.dtype(dtype))
        args.append(nc.dram_tensor(f"out_{i}_dram", shape, dt, kind="ExternalOutput").ap())
    build(nc, *args)
    r = _run(nc, [arrays], core_ids=[0])
    return tuple(r.results[0][f"out_{i}_dram"] for i in range(len(_OUTS)))
```

```python
from contextlib import ExitStack

import concourse.bass as bass
from concourse import mybir

ALU = mybir.AluOpType
ACT = mybir.ActivationFunctionType
F32 = mybir.dt.float32
BF16 = mybir.dt.bfloat16
I32 = mybir.dt.int32
U32 = mybir.dt.uint32
X = mybir.AxisListType.X
XY = mybir.AxisListType.XY

P = 128
D = 1024
DC = D // P
G = 512
H = 4
NT = 16
NMETA = 16
NS = 8
TR = NMETA + NS
NPG = 64
HC = 2 * H
EPS = 1e-6
LAM0 = 0.8 - 0.6
BIG = 1e30
SLOTS = 8
READ = 4
ORDER_A = "K0 V0 V1 K1 K2 K3 K4 K5 V2 V3 K6 V4 V5 K7 V6 V7".split()
ORDER_B = "K0 V0 V1 K1 K2 K3 K4 K5 V2 V3 K6 V4 V5 K7 V6 V7".split()
ORDER_K = [f"K{s}" for s in range(SLOTS)]
ORDER_TAIL = [f"V{s}" for s in range(SLOTS)]
RSQRT_SEED = 1597463007.0
RS_STEPS = 11


def blocks_before(g, r):
    return 16 * g * (g + 1) + r * (8 * (g + 1))


class Chain:

    def __init__(self, eng, sem):
        self.eng, self.sem, self.base, self.r, self.per, self.n, self.first = eng, sem, 0, 0, 0, 0, 0

    def enter(self, first, per):
        self.first, self.base, self.per, self.n = first, self.base - first * per, per, 0

    def leave(self, times):
        assert self.n == self.per, f"chain: {self.n} steps, declared {self.per}"
        self.base, self.r, self.per, self.n = self.base + (self.first + times) * self.n, 0, 0, 0

    def flat(self):
        self.base, self.r, self.per, self.n = self.base + self.n, 0, 0, 0

    def __call__(self, ins):
        self.n += 1
        ins.then_inc(self.sem, 1)
        self.eng.wait_ge(self.sem, self.base + self.r * self.per + self.n)


TWO_FREE = 2
FOUR_FREE = 4
ONE_ON = 1
SU_BANK = 2
BANK = (0, 1, 3, 2)
OUT_SLOTS = 4


def after(value, free):
    return value + free


def need(eng, sem, value):
    if isinstance(value, int) and value <= 0:
        return
    eng.wait_ge(sem, value)


def build(nc, x_prompt, x_sample, cache_k, cache_v, state_hgrn, page_table, meta_tokens, norm_w, w_in, w_out,
          lb_logits, hgrn_norm_w, subln_w, lam_q1, lam_k1, lam_q2, lam_k2, final_norm_w,
          y_prompt, y_sample, new_k_prompt, new_v_prompt, new_state_prompt,
          new_k_sample, new_v_sample, new_state_sample):
    xp = x_prompt[0]
    xs = x_sample.rearrange("b t d -> (b t) d")
    yp = y_prompt[0]
    ys = y_sample.rearrange("b t d -> (b t) d")
    kc = cache_k[0].rearrange("g t h d -> g t (h d)")
    vc = cache_v[0].rearrange("g t h d -> g t (h d)")
    nkp = new_k_prompt[0, 0].rearrange("t h d -> t (h d)")
    nvp = new_v_prompt[0, 0].rearrange("t h d -> t (h d)")
    nks = new_k_sample[0].rearrange("b t h d -> (b t) (h d)")
    nvs = new_v_sample[0].rearrange("b t h d -> (b t) (h d)")
    pages = page_table.rearrange("b (a n) -> a (b n)", a=1)
    win = w_in[0].rearrange("(c p) n -> p c n", p=P)
    wout = w_out[0].rearrange("(c p) n -> p c n", p=P)
    s_in = state_hgrn[0].rearrange("b h c v -> c (b h) v")
    s_out = new_state_sample[0].rearrange("b h c v -> c (b h) v")
    sp_out = new_state_prompt[0, 0].rearrange("h c v -> c h v")
    y_att_dram = nc.dram_tensor("y_att_scratch", (NT, P, G), F32, kind="Internal").ap()

    with ExitStack() as ctx:
        def sb(name, shape, dt=F32):
            return ctx.enter_context(nc.sbuf_tensor(name, shape, dt))

        def sem(name):
            return ctx.enter_context(nc.semaphore(name))

        ident = sb("ident", [P, P])
        identb = sb("identb", [P, P], BF16)
        causal = sb("causal", [P, 896], BF16)
        normw = sb("normw", [P, D])
        subw = sb("subw", [P, P])
        hgw = sb("hgw", [P, P])
        ones = sb("ones", [P, P])
        pick = sb("pick", [P, 2 * TR - 1])
        zero8 = sb("zero8", [P, 8])
        start = sb("start", [P, 14])
        hmask = sb("hmask", [P, H])
        sgn = sb("sgn", [P, 1])
        nlam = sb("nlam", [P, 1])
        lamr = sb("lamr", [P, 4, 64])
        lamw = sb("lamw", [P, 8])
        lbl = sb("lbl", [P, H])
        lbw = sb("lbw", [P, 4, H])
        selm = sb("selm", [P, NS])
        W = sb("W", [P, 4, DC, G])
        xbuf = sb("xbuf", [P, D])
        U = sb("U", [P, D])
        xT = sb("xT", [P, DC, P])
        gw = sb("gw", [P, G])
        ssx = sb("ssx", [P, 2])
        rsb = sb("rsb", [P, 3, 4])
        qX = sb("qX", [P, G])
        vX = sb("vX", [P, G])
        gwX = sb("gwX", [P, G])
        oX = sb("oX", [P, G])
        sNew = sb("sNew", [P, HC])
        Kt = sb("Kt", [P, 2, 2, G])
        Vt = sb("Vt", [P, 2, 2, G])
        qb = sb("qb", [P, G])
        sc = sb("sc", [P, 2, NPG + 1, HC])
        pst = sb("pst", [P, 16 * HC])
        mpart = sb("mpart", [P, HC])
        mx8 = sb("mx8", [HC, 1])
        mxd = sb("mxd", [HC, HC])
        psums = sb("psums", [P, HC])
        srep = sb("srep", [P, P])
        coefD = sb("coefD", [P, 2])
        tmpD = sb("tmpD", [P, G])
        Qz = sb("Qz", [P, 2, H, P])
        Pb = sb("Pb", [P, 4, G])
        P4 = sb("P4", [P, 16])
        PTs = sb("PTs", [P, 2, G])
        oh = sb("oh", [P, G])
        negm = sb("negm", [P, 2, 2])
        sums = sb("sums", [P, 2, 5])
        rcp = sb("rcp", [P, 2])
        ssO = sb("ssO", [P, H])
        KTW = H * (NT * P + NMETA)
        region = sb("region", [P, KTW + NT * G])
        KT = region[:, 0:KTW].rearrange("p (h t) -> p h t", h=H)
        V = region[:, KTW:KTW + NT * G].rearrange("p (t n) -> p t n", t=NT)
        at = [0]

        def part(n):
            at[0] += n
            assert at[0] <= KTW + NT * G
            return region[:, at[0] - n:at[0]]

        Wo = part(DC * D).rearrange("p (c n) -> p c n", c=DC)
        fw = part(D)
        ycat = part(D)
        hbuf = part(D)
        yTs = part(D).rearrange("p (c t) -> p c t", c=DC)
        masks = part(8 * P).rearrange("p (l t) -> p l t", l=8)
        S_ = part(G)
        qT = part(G)
        kT = part(G)
        PP = part(G)
        QQ = part(G)
        Xl = [part(G), sb("Xl1", [P, G])[:, :]]
        Am = sb("Am", [P, G])[:, :]
        XQ = Qz[:, 0, :, :].rearrange("p h t -> p (h t)")
        Pflat = Pb[:, :, :].rearrange("p a n -> p (a n)")
        XK = Pflat[:, 0:G]
        ib = Pflat[:, G:2 * G]
        kd = Pflat[:, 2 * G:3 * G]
        QM = Qz[:, :, :, :].rearrange("p a h t -> p (a h t)")[:, 0:H * NS * TR].rearrange("p (h n) -> p h n", h=H)
        AX = PTs[:, 0, 0:H * TR].rearrange("p (h t) -> p h t", h=H)
        qPX = PTs[:, 0, H * TR:2 * H * TR].rearrange("p (h t) -> p h t", h=H)
        fX = PTs[:, 0, 2 * H * TR:3 * H * TR].rearrange("p (h t) -> p h t", h=H)
        kX = Pflat[:, 3 * G:4 * G]
        kmX = [PTs[:, 1, :], tmpD[:, :]]
        SX = W[:, 0, :, :].rearrange("p c n -> p (c n)").rearrange("p (s v) -> p s v", v=P)

        PS = ctx.enter_context(nc.psum_tensor("PS", [P, 4, G], F32))
        PT = ctx.enter_context(nc.psum_tensor("PT", [P, 2, G], F32))
        PO = ctx.enter_context(nc.psum_tensor("PO", [P, G], F32))
        PD = ctx.enter_context(nc.psum_tensor("PD", [P, G], F32))

        const_in = sem("const_in"); norm_in = sem("norm_in"); made = sem("made"); cst = sem("cst"); lam_e = sem("lam_e"); cst2 = sem("cst2")
        wA = [sem(f"wA{n}") for n in range(4)]; wB = sem("wB"); wO = sem("wO")
        x_loaded = sem("x_loaded"); ss_ready = sem("ss_ready"); xn_ready = sem("xn_ready")
        x_tr = sem("x_tr"); xT_ready = sem("xT_ready"); proj = sem("proj")
        q_ev = sem("q_ev"); k_ev = sem("k_ev"); v_ev = sem("v_ev"); th_ev = sem("th_ev"); g_ev = sem("g_ev")
        qk_tr = sem("qk_tr"); qT_ev = sem("qT_ev"); kT_ev = sem("kT_ev")
        k_st = sem("k_st"); v_st = sem("v_st"); 
        S_done = sem("S_done"); m_ready = sem("m_ready"); P_ready = sem("P_ready"); P_tr = sem("P_tr")
        PT_ev = sem("PT_ev"); PV_done = sem("PV_done"); post = sem("post"); ssO_ready = sem("ssO_ready")
        y_ready = sem("y_ready"); qX_tr = sem("qX_tr"); dve = sem("dve")
        k_load = [sem("k_load0"), sem("k_load1")]; v_load = [sem("v_load0"), sem("v_load1")]
        k_used = sem("k_used"); v_used = sem("v_used"); pst_ready = sem("pst_ready")
        d_om = sem("d_om"); d_cmb = sem("d_cmb"); d_mx = sem("d_mx"); d_row = sem("d_row"); d_mxT = sem("d_mxT"); d_mxd = sem("d_mxd")
        d_mb = sem("d_mb"); d_sub = sem("d_sub"); d_exp = sem("d_exp"); d_sr = sem("d_sr"); d_L = sem("d_L")
        d_qm = sem("d_qm"); d_qb = sem("d_qb"); d_lread = sem("d_lread"); d_end = sem("d_end"); d_v1 = sem("d_v1")
        z_ev = sem("z_ev"); kf = sem("kf"); x_lev = sem("x_lev"); a_lev = sem("a_lev"); a_cp = sem("a_cp")
        kd_tr = sem("kd_tr"); kd_ev = sem("kd_ev"); o_done = sem("o_done"); su = sem("su"); s_upd = sem("s_upd")
        ssR = sem("ssR"); yB = sem("yB"); y_tr = sem("y_tr"); yT_ev = sem("yT_ev"); h_mm = sem("h_mm")
        h_add = sem("h_add"); ssH = sem("ssH"); y_out = sem("y_out"); yb_st = sem("yb_st"); ya_load = sem("ya_load")
        hx_load = sem("hx_load"); b_made = sem("b_made"); st_in = sem("st_in"); t_dve = sem("t_dve")
        t_pe = sem("t_pe"); t_act = sem("t_act"); st_out = sem("st_out"); bconst = sem("bconst"); b_init = sem("b_init")

        block = ctx.enter_context(nc.Block())
        KALL = NT + 1

        def load_x(eng, dst, s, t):
            if isinstance(t, int) and t == 0:
                eng.dma_start(dst[0:16, :], meta_tokens).then_inc(s, 16)
                eng.dma_start(dst[16:P, :], xp[0:112, :]).then_inc(s, 16)
            elif isinstance(t, int):
                eng.dma_start(dst[0:16, :], xp[t * P - 16:t * P, :]).then_inc(s, 16)
                eng.dma_start(dst[16:P, :], xp[t * P:t * P + 112, :]).then_inc(s, 16)
            else:
                eng.dma_start(dst[0:16, :], xp[bass.ds(t * P - 16, 16), :]).then_inc(s, 16)
                eng.dma_start(dst[16:P, :], xp[bass.ds(t * P, 112), :]).then_inc(s, 16)

        def load_tail(eng, dst, s):
            eng.dma_start(dst[0:16, :], xp[NT * P - 16:NT * P, :]).then_inc(s, 16)
            eng.dma_start(dst[16:TR, :], xs).then_inc(s, 16)

        @block.sync
        def _(sp):
            def page_numbers(index, count):
                _, numbers = nc.values_load_multi_w_load_instructions(
                    pages[:, bass.ds(index, count)], engines=[mybir.EngineType.SP], min_val=0, max_val=kc.shape[0] - 1)
                return numbers

            def page_pair(cache, dst, pair, s, free, uses):
                need(sp, free, uses)
                for u, page in enumerate(pair):
                    sp.dma_start(dst[:, u, :], cache[bass.ds(page, 1), :, :].rearrange("a t n -> t (a n)")).then_inc(s, 16)

            def slots(it, order):
                for slot in order:
                    s = int(slot[1])
                    u = 2 * (s % READ)
                    if slot[0] == "K":
                        if s % READ == 0:
                            keys = page_numbers(16 * it + 2 * s, 2 * READ)
                        page_pair(kc, Kt[:, s % 2], keys[u:u + 2], k_load[s % 2], k_used, after(8 * it + (s - 1), TWO_FREE))
                    elif order is ORDER_TAIL:
                        if s % READ == 0:
                            values = page_numbers(16 * (it - 4) + 2 * s, 2 * READ)
                        ring, loaded = ((Vt, v_load), (Kt, k_load))[s // 2 % 2]
                        page_pair(vc, ring[:, s % 2], values[u:u + 2], loaded[s % 2], v_used, after(4 * (it - 4) + s // 2 - 1, ONE_ON))
                    else:
                        if s % READ == 0:
                            values = page_numbers(16 * (it - 4) + 2 * s, 2 * READ)
                        page_pair(vc, Vt[:, s % 2], values[u:u + 2], v_load[s % 2], v_used, after(4 * (it - 4) + s // 2, ONE_ON))

            sp.wait_ge(made, 1)
            load_tail(sp, xbuf, x_loaded)
            sp.dma_start(normw[:, :], norm_w.partition_broadcast(P).rearrange("p a d -> p (a d)")).then_inc(norm_in, 16)
            sp.dma_start(subw[:, :], subln_w.partition_broadcast(P).rearrange("p a d -> p (a d)")).then_inc(const_in, 16)
            sp.dma_start(hgw[:, :], hgrn_norm_w.partition_broadcast(P).rearrange("p a d -> p (a d)")).then_inc(const_in, 16)
            for n, a in enumerate((lam_q1, lam_k1, lam_q2, lam_k2)):
                sp.dma_start(lamr[:, n, :], a.partition_broadcast(P).rearrange("p a d -> p (a d)")).then_inc(const_in, 16)
            with nc.allow_non_contiguous_dma(reason="512 lower-bound logits, channel on partition"):
                sp.dma_start(lbl[:, :], lb_logits.rearrange("a (h c) -> c (a h)", c=P)).then_inc(const_in, 16)
            sp.wait_ge(xn_ready, 1)
            load_x(sp, xbuf, x_loaded, 0)
            with sp.Fori(0, 4) as it:
                need(sp, xn_ready, it + 2)
                load_x(sp, xbuf, x_loaded, it + 1)
                slots(it, ORDER_K)
            with sp.Fori(4, NT - 1) as it:
                need(sp, xn_ready, it + 2)
                load_x(sp, xbuf, x_loaded, it + 1)
                slots(it, ORDER_A)
            sp.wait_ge(xn_ready, NT + 1)
            load_x(sp, xbuf, x_loaded, 0)
            slots(NT - 1, ORDER_A)

            with sp.Fori(0, NT - 1) as t:
                need(sp, xn_ready, t + KALL + 1)
                load_x(sp, xbuf, x_loaded, t + 1)
                slots(t + NT, ORDER_B)
            sp.wait_ge(xn_ready, 2 * KALL - 1)
            load_tail(sp, xbuf, x_loaded)
            slots(2 * NT - 1, ORDER_B)
            sp.wait_ge(k_used, after(8 * 2 * NT, TWO_FREE))
            slots(2 * NT, ORDER_TAIL)
            sp.wait_ge(proj, 4 * (2 * KALL))
            sp.dma_start(SX, s_in).then_inc(st_in, 16)
            with sp.Fori(2 * NT + 1, 2 * NT + 4) as it:
                slots(it, ORDER_TAIL)
            sp.wait_ge(t_dve, 4)
            sp.dma_start(s_out, SX).then_inc(st_out, 16)
            sp.dma_start(sp_out, S_.rearrange("p (h v) -> p h v", h=H)).then_inc(st_out, 16)
            sp.wait_ge(y_out, NT + 1)
            sp.dma_start(yp[NT * P - 16:NT * P, :], hbuf[0:16, :]).then_inc(st_out, 16)
            sp.dma_start(ys, hbuf[16:TR, :]).then_inc(st_out, 16)
            sp.wait_ge(st_out, 64)
            sp.wait_ge(k_st, 32 + 16 * NT)
            sp.wait_ge(v_st, 32 + 32 * NT)

        @block.gpsimd
        def _(pool):
            pool.memset(xbuf[:, :], 0.0).then_inc(made, 1)
            pool.memset(ident[:, :], 0.0).then_inc(made, 1)
            pool.memset(causal[:, :], 0.0).then_inc(made, 1)
            pool.wait_ge(made, 3)
            pool.affine_select(out=ident[:, :], in_=ident[:, :], compare_op=ALU.not_equal, fill=1.0, base=0,
                               pattern=[[-1, P]], channel_multiplier=1).then_inc(made, 1)
            pool.affine_select(out=causal[:, :], in_=causal[:, :], compare_op=ALU.is_ge, fill=-BIG, base=384,
                               pattern=[[-1, 896]], channel_multiplier=1).then_inc(made, 1)
            pool.memset(ones[:, :], 1.0).then_inc(made, 1)
            pool.memset(srep[:, :], 1.0).then_inc(made, 1)
            pool.memset(pick[:, :], 0.0).then_inc(made, 1)
            pool.memset(zero8[:, :], 0.0).then_inc(made, 1)
            pool.memset(Qz[:, :, :, :], 0.0).then_inc(made, 1)
            pool.wait_ge(made, 10)
            pool.memset(pick[:, TR - 1:TR], 1.0).then_inc(made, 1)
            pool.memset(region[:, :], 0.0).then_inc(made, 1)
            pool.wait_ge(k_ev, 1)
            pool.dma_start(nkp[NT * P:NT * P + 16, :], U[0:16, G:D]).then_inc(k_st, 16)
            pool.dma_start(nks, U[16:TR, G:D]).then_inc(k_st, 16)
            pool.wait_ge(v_ev, 1)
            pool.dma_start(nvp[NT * P:NT * P + 16, :], vX[0:16, :]).then_inc(v_st, 16)
            pool.dma_start(nvs, vX[16:TR, :]).then_inc(v_st, 16)
            with pool.Fori(0, NT) as it:
                pool.wait_ge(k_ev, it + 2)
                pool.dma_start(nkp[bass.ds(it * P, P), :], U[:, G:D]).then_inc(k_st, 16)
                pool.wait_ge(v_ev, it + 2)
                pool.dma_start(nvp[bass.ds(it * P, P), :],
                               V[:, bass.ds(it, 1), :].rearrange("p a n -> p (a n)")).then_inc(v_st, 16)
                pool.wait_ge(y_ready, after(it + 1, ONE_ON))
                pool.dma_start(y_att_dram[bass.ds(it, 1), :, :].rearrange("a p n -> p (a n)"), oh[:, :]).then_inc(v_st, 16)
            for n in range(4):
                if n == 0:
                    pool.wait_ge(proj, 4 * KALL)
                pool.dma_start(W[:, n], win[:, :, n * G:(n + 1) * G]).then_inc(wB, 16)
            pool.wait_ge(P_tr, after(blocks_before(4, 0) + 40, ONE_ON))
            pool.wait_ge(PV_done, after(blocks_before(4, 0) + 40, TWO_FREE))
            pool.wait_ge(v_st, 32 + 32 * NT)
            pool.dma_start(Wo, wout).then_inc(wO, 16)
            pool.dma_start(fw, final_norm_w.rearrange("(a d) -> a d", a=1).partition_broadcast(P)
                           .rearrange("p a d -> p (a d)")).then_inc(wO, 16)
            load_x(pool, hbuf, hx_load, 0)
            pool.dma_start(ycat[:, G:D], y_att_dram[0]).then_inc(ya_load, 16)
            pool.memset(masks[:, 1:8, :], 0.0).then_inc(b_made, 1)
            pool.memset(S_, 0.0).then_inc(b_made, 1)
            pool.memset(Am, 0.0).then_inc(b_made, 1)
            pool.wait_ge(b_made, 3)
            for l in range(1, 8):
                m = 1 << (l - 1)
                pool.memset(masks[:, l, :].rearrange("p (j two m) -> p j two m", two=2, m=m)[:, :, 1, :], 1.0).then_inc(b_made, 1)
            pool.wait_ge(b_made, 10)
            for l in range(1, 8):
                m = 1 << (l - 1)
                v = masks[:, l, :].rearrange("p (j two m) -> p j two m", two=2, m=m)[:, :, 1, :]
                nj = P // (2 * m)
                pool.affine_select(out=v, in_=v, compare_op=ALU.is_ge, fill=0.0, base=0,
                                   pattern=[[-2 * m, nj], [0, m]], channel_multiplier=1).then_inc(b_made, 1)
            pool.wait_ge(b_made, 17)
            for l in range(1, 8):
                m = 1 << (l - 1)
                v = masks[:, l, :].rearrange("p (j two m) -> p j two m", two=2, m=m)[:, :, 1, :]
                nj = P // (2 * m)
                pool.affine_select(out=v, in_=v, compare_op=ALU.is_ge, fill=0.0, base=m - 1,
                                   pattern=[[2 * m, nj], [0, m]], channel_multiplier=-1).then_inc(b_made, 1)
            pool.wait_ge(y_tr, 2)
            pool.dma_start(ycat[:, G:D], y_att_dram[1]).then_inc(ya_load, 16)
            pool.wait_ge(y_out, 1)
            pool.dma_start(yp[0:112, :], hbuf[16:P, :]).then_inc(yb_st, 16)
            pool.wait_ge(yb_st, 16)
            load_x(pool, hbuf, hx_load, 1)
            with pool.Fori(1, NT - 1) as t:
                pool.wait_ge(y_tr, 2 * t + 2)
                pool.dma_start(ycat[:, G:D], y_att_dram[bass.ds(t + 1, 1), :, :].rearrange("a p n -> p (a n)")).then_inc(ya_load, 16)
                pool.wait_ge(y_out, t + 1)
                pool.dma_start(yp[bass.ds(t * P - 16, 16), :], hbuf[0:16, :]).then_inc(yb_st, 16)
                pool.dma_start(yp[bass.ds(t * P, 112), :], hbuf[16:P, :]).then_inc(yb_st, 16)
                pool.wait_ge(yb_st, t * 32 + 16)
                load_x(pool, hbuf, hx_load, t + 1)
            pool.wait_ge(y_out, NT)
            t = NT - 1
            pool.dma_start(yp[t * P - 16:t * P, :], hbuf[0:16, :]).then_inc(yb_st, 16)
            pool.dma_start(yp[t * P:t * P + 112, :], hbuf[16:P, :]).then_inc(yb_st, 16)
            pool.wait_ge(yb_st, 32 * NT - 16)
            load_tail(pool, hbuf, hx_load)

        @block.scalar
        def _(act):
            act.wait_ge(x_loaded, 32)
            act.wait_ge(norm_in, 16)
            for n in (1, 0, 3, 2):
                act.dma_start(W[:, n], win[:, :, 4 * G + n * G:4 * G + (n + 1) * G]).then_inc(wA[n], 16)
            xT_flat = xT[:, :, :].rearrange("p c t -> p (c t)")

            def square_x(n):
                act.wait_ge(x_loaded, 32 * (n + 1))
                need(act, proj, 4 * n)
                act.activation(xT_flat, xbuf[:, :], ACT.Square, accum_out=ssx[:, 0:1]).then_inc(ss_ready, 1)

            def xT_out(n):
                for a in range(2):
                    act.wait_ge(x_tr, 2 * n + a + 1)
                    act.activation(xT[:, 4 * a:4 * a + 4, :].rearrange("p c t -> p (c t)"), PT[:, a, :],
                                   ACT.Copy).then_inc(xT_ready, 1)

            def stage_p(it, g):
                if g == 0:
                    return
                act.wait_ge(d_exp, g)
                need(act, v_used, after(4 * (it - 4), ONE_ON))
                act.activation(pst[:, :], sc[:, (g - 1) % 2, bass.ds((it - 4 * g) * 16, 16), :]
                               .rearrange("p a c -> p (a c)"), ACT.Copy).then_inc(pst_ready, 1)

            def exp_blocks(i, it8, base, nb, tail=False, narrow=False):
                act.wait_ge(m_ready, it8 + i + 1)
                for j in range(nb):
                    depth = 2 if nb == 1 else 1
                    place = i % 2 if nb == 1 else j
                    need(act, P_tr, after(base + ((i - depth) * nb + j + 1 if i >= depth else 0), ONE_ON))
                    if tail and j == 4:
                        src, dst = PD[:, 0:16], P4[:, :]
                    else:
                        src, dst = PS[:, place, :], Pb[:, place, :]
                    if narrow and j == nb - 1:
                        src, dst = src[:, 0:P], dst[:, 0:P]
                    act.activation(dst, src, ACT.Exp, bias=negm[:, i % 2, 0:1],
                                   accum_out=sums[:, i % 2, j:j + 1]).then_inc(P_ready, 1)

            def evac_blocks(i, base, nb, tail=False, narrow=False):
                for j in range(nb):
                    n = i * nb + j
                    act.wait_ge(P_tr, after(base + (n + 1), ONE_ON))
                    need(act, PV_done, after(base + (n - 1), TWO_FREE))
                    if tail and j == 4:
                        act.activation(PTs[0:16, n % 2, 0:P], PT[0:16, n % 2, 0:P], ACT.Copy).then_inc(PT_ev, 1)
                    else:
                        w = P if narrow and j == nb - 1 else G
                        act.activation(PTs[:, n % 2, 0:w], PT[:, n % 2, 0:w], ACT.Copy).then_inc(PT_ev, 1)

            def d_exponent(k):
                if 1 <= k <= NS:
                    act.wait_ge(d_sub, k)
                    v = sc[:, (k - 1) % 2, :, :].rearrange("p a c -> p (a c)")
                    act.activation(v, v, ACT.Exp).then_inc(d_exp, 1)

            square_x(0)
            xT_out(0)
            act.wait_ge(cst, 1)
            act.activation(lamw[:, 2:4], lamw[:, 0:2], ACT.Exp).then_inc(lam_e, 1)
            act.activation(lbw[:, 1, :], lbw[:, 0, :], ACT.Exp).then_inc(lam_e, 1)
            act.wait_ge(proj, 2)
            act.activation(qX[0:TR, :], PS[0:TR, 0, :], ACT.Copy, scale=0.125).then_inc(q_ev, 1)
            act.wait_ge(proj, 3)
            act.activation(gwX[0:TR, :], PS[0:TR, BANK[3], :], ACT.Tanh, scale=0.5).then_inc(th_ev, 1)
            act.wait_ge(proj, 4)
            act.activation(vX[0:TR, :], PS[0:TR, BANK[2], :], ACT.Copy).then_inc(v_ev, 1)
            square_x(1)
            xT_out(1)

            def a_tile(it, g, r):
                n = it + 1
                base = blocks_before(g, r)
                nb = g + 1
                narrow = isinstance(r, int)
                stage_p(it, g)
                act.wait_ge(proj, 4 * n + 2)
                act.activation(U[:, 0:G], PS[:, 0, :], ACT.Copy, scale=0.125).then_inc(q_ev, 1)
                act.wait_ge(proj, 4 * n + 3)
                need(act, y_ready, after(it + 0, ONE_ON))
                act.activation(gw[:, :], PS[:, BANK[3], :], ACT.Tanh, scale=0.5).then_inc(th_ev, 1)
                act.wait_ge(qk_tr, 2 * n + 1)
                for c in range(2):
                    rows = slice(64 * c, 64 * c + 64)
                    last = act.activation(Qz[rows, c, :, :].rearrange("p h t -> p (h t)"), PT[rows, 0, :], ACT.Copy)
                last.then_inc(qT_ev, 1)
                if nb < 4:
                    exp_blocks(0, 8 * it, base, nb, narrow=narrow)
                act.wait_ge(proj, 4 * n + 4)
                act.activation(V[:, bass.ds(it, 1), :].rearrange("p a n -> p (a n)"), PS[:, BANK[2], :], ACT.Copy).then_inc(v_ev, 1)
                if nb == 4:
                    exp_blocks(0, 8 * it, base, nb, narrow=narrow)
                if nb == 1:
                    exp_blocks(1, 8 * it, base, nb, narrow=narrow)
                for i in range(1, 8):
                    evac_blocks(i - 1, base, nb, narrow=narrow)
                    if nb > 1:
                        exp_blocks(i, 8 * it, base, nb, narrow=narrow)
                    elif i < 7:
                        exp_blocks(i + 1, 8 * it, base, nb, narrow=narrow)
                    if i == 3:
                        square_x(n + 1)
                xT_out(n + 1)
                evac_blocks(7, base, nb, narrow=narrow)
                act.wait_ge(post, after(8 * it + 8, FOUR_FREE))
                for h in range(H):
                    last = act.activation(Pb[:, 0, h * P:(h + 1) * P], oh[:, h * P:(h + 1) * P], ACT.Square, accum_out=ssO[:, h:h + 1])
                last.then_inc(ssO_ready, 1)
                act.wait_ge(ssO_ready, it + 1)

            for g in range(4):
                d_exponent(g)
                a_tile(4 * g, g, 0)
                with act.Fori(1, 4) as r:
                    a_tile(4 * g + r, g, r)
            base = blocks_before(4, 0)
            act.wait_ge(qX_tr, 1)
            for c in range(2):
                rows = slice(64 * c, 64 * c + 64)
                last = act.activation(Qz[rows, c, :, 0:TR], PT[rows, 0, 0:H * TR].rearrange("p (h t) -> p h t", h=H), ACT.Copy)
            last.then_inc(qT_ev, 1)
            exp_blocks(0, 8 * NT, base, 5, tail=True)
            for i in range(1, 8):
                evac_blocks(i - 1, base, 5, tail=True)
                exp_blocks(i, 8 * NT, base, 5, tail=True)
            evac_blocks(7, base, 5, tail=True)

            def yT_out(t, rows=P):
                for a in range(2):
                    act.wait_ge(y_tr, 2 * t + (a + 1))
                    act.activation(yTs[:, 4 * a:4 * a + 4, 0:rows], PT[:, a, 0:4 * rows].rearrange("p (c t) -> p c t", c=4),
                                   ACT.Copy).then_inc(yT_ev, 1)

            def square_h(t, junk, rows=P):
                act.wait_ge(h_add, after(t + 1, ONE_ON))
                act.activation(junk[0:rows, :], hbuf[0:rows, :], ACT.Square, accum_out=ssx[0:rows, 1:2]).then_inc(ssH, 1)

            def b_tile(t, g, first=False):
                it = t + NT
                n = t + KALL
                stage_p(it, g)
                act.wait_ge(proj, 4 * n + 2)
                act.activation(U[:, 0:G], PS[:, 0, :], ACT.Copy).then_inc(q_ev, 1)
                act.wait_ge(proj, 4 * n + 3)
                act.wait_ge(y_ready, after(NT, ONE_ON))
                need(act, yB, after(t + 0, ONE_ON))
                act.activation(gw[:, :], PS[:, BANK[3], :], ACT.Tanh, scale=0.5).then_inc(th_ev, 1)
                act.wait_ge(qk_tr, 2 * n + 1)
                need(act, x_lev, after(8 * t, ONE_ON))
                need(act, s_upd, after(t + 0, ONE_ON))
                act.activation(qT, PT[:, 0, :], ACT.Copy).then_inc(qT_ev, 1)
                act.wait_ge(qk_tr, 2 * n + 2)
                act.activation(PP, PT[:, 1, :], ACT.Tanh, scale=0.5).then_inc(z_ev, 1)
                act.wait_ge(proj, 4 * n + 4)
                act.activation(ib, PS[:, BANK[2], :], ACT.Copy).then_inc(v_ev, 1)
                square_x(n + 1)
                if not first:
                    yT_out(t - 1)
                xT_out(n + 1)
                act.wait_ge(kd_tr, t + 1)
                act.activation(kd, PT[:, 0, :], ACT.Copy).then_inc(kd_ev, 1)
                act.wait_ge(o_done, t + 1)
                for h in range(H):
                    last = act.activation(oh[:, h * P:(h + 1) * P], PO[:, h * P:(h + 1) * P], ACT.Square, accum_out=ssO[:, h:h + 1])
                last.then_inc(ssR, 1)
                if not first:
                    square_h(t - 1, oh_wide)

            oh_wide = PTs[:, :, :].rearrange("p a n -> p (a n)")
            for g in range(4, 8):
                d_exponent(g)
                b_tile(4 * (g - 4), g, first=(g == 4))
                with act.Fori(1, 4) as r:
                    b_tile(4 * (g - 4) + r, g)
            d_exponent(8)
            n = 2 * KALL - 1
            stage_p(2 * NT, 8)
            act.wait_ge(proj, 4 * n + 2)
            act.activation(U[0:TR, 0:G], PS[0:TR, 0, :], ACT.Copy).then_inc(q_ev, 1)
            act.wait_ge(proj, 4 * n + 3)
            act.wait_ge(yB, after(NT, ONE_ON))
            act.wait_ge(x_lev, after(8 * NT, ONE_ON))
            act.wait_ge(s_upd, after(NT, ONE_ON))
            act.activation(gw[0:TR, :], PS[0:TR, BANK[3], :], ACT.Tanh, scale=0.5).then_inc(th_ev, 1)
            act.wait_ge(qk_tr, 2 * n + 1)
            act.activation(qT[:, 0:H * TR], PT[:, 0, 0:H * TR], ACT.Copy).then_inc(qT_ev, 1)
            act.wait_ge(qk_tr, 2 * n + 2)
            act.activation(PP[:, 0:H * TR], PT[:, 1, 0:H * TR], ACT.Tanh, scale=0.5).then_inc(z_ev, 1)
            act.wait_ge(proj, 4 * n + 4)
            act.activation(ib[0:TR, :], PS[0:TR, BANK[2], :], ACT.Copy).then_inc(v_ev, 1)
            yT_out(NT - 1)
            stage_p(2 * NT + 1, 8)
            square_h(NT - 1, xT_flat)
            act.wait_ge(t_pe, 1)
            act.activation(kd[0:16, :], PT[0:16, 0, :], ACT.Copy).then_inc(t_act, 1)
            act.activation(kX[0:TR, :], PT[0:TR, 1, :], ACT.Copy).then_inc(t_act, 1)
            stage_p(2 * NT + 2, 8)
            act.wait_ge(o_done, NT + 1)
            for h in range(H):
                last = act.activation(oh[0:TR, h * P:(h + 1) * P], PO[0:TR, h * P:(h + 1) * P], ACT.Square,
                                      accum_out=ssO[0:TR, h:h + 1])
            last.then_inc(ssR, 1)
            stage_p(2 * NT + 3, 8)
            act.wait_ge(t_dve, 5)
            for h in range(H):
                last = act.activation(oh[0:TR, h * P:(h + 1) * P], oX[0:TR, h * P:(h + 1) * P], ACT.Square,
                                      accum_out=ssO[0:TR, h:h + 1])
            last.then_inc(ssR, 1)
            yT_out(NT, TR)
            square_h(NT, xT_flat, TR)

        @block.vector
        def _(ve):
            link = Chain(ve, dve)

            def rsqrt(dst, ss, inv_n):
                w = ss.shape[-1]
                rows = ss.shape[0]
                y, xh, t = dst, rsb[0:rows, 1, 0:w], rsb[0:rows, 2, 0:w]
                link(ve.tensor_scalar(xh, ss, inv_n, EPS, ALU.mult, ALU.add))
                link(ve.tensor_scalar(y.bitcast(I32), xh.bitcast(I32), -0.5, RSQRT_SEED, ALU.mult, ALU.add))
                for _ in range(3):
                    link(ve.scalar_tensor_tensor(out=t, in0=y, scalar=-0.5, in1=y, op0=ALU.mult, op1=ALU.mult))
                    link(ve.tensor_tensor(t, t, xh, ALU.mult))
                    link(ve.scalar_tensor_tensor(out=y, in0=t, scalar=1.5, in1=y, op0=ALU.add, op1=ALU.mult))

            rs = rsb[:, 0, :]

            def norm_x(n):
                ve.wait_ge(ss_ready, n + 1)
                rsqrt(rs[:, 0:1], ssx[:, 0:1], 1.0 / D)
                need(ve, qk_tr, 2 * n)
                ve.scalar_tensor_tensor(out=U[:, :], in0=xbuf[:, :], scalar=rs[:, 0:1], in1=normw[:, :],
                                        op0=ALU.mult, op1=ALU.mult).then_inc(xn_ready, 1)

            def gate(n, dst, w4, rows=P):
                ve.wait_ge(th_ev, n + 1)
                link(ve.scalar_tensor_tensor(out=dst, in0=dst, scalar=1.0, in1=PS[0:rows, BANK[3], :], op0=ALU.add, op1=ALU.mult))
                d3 = dst.rearrange("p (h d) -> p h d", h=H)
                ve.tensor_tensor(d3, d3, w4[0:rows, :].unsqueeze(1).to_broadcast([rows, H, P]), ALU.mult).then_inc(g_ev, 1)

            def key_slot(it, s, g):
                ve.wait_ge(k_load[s % 2], (it * 4 + (s // 2 + 1)) * 32)
                kp = Kt[:, s % 2]
                link(ve.tensor_tensor(kp, kp, qb[:, :].unsqueeze(1).to_broadcast([P, 2, G]), ALU.mult))
                r16 = (it - 4 * g) * 16 + 2 * s
                ve.tensor_reduce(sc[:, g % 2, bass.ds(r16, 2), :].rearrange("p a c -> p (a c)"),
                                 kp.rearrange("p a (c d) -> p (a c) d", d=64), X, ALU.add).then_inc(k_used, 1)

            def d_query(k):
                if k < NS:
                    need(ve, d_cmb, k - 2)
                    ve.tensor_scalar(tmpD[0:TR, :], qX[0:TR, :], ident[0:TR, 16 + k:17 + k], None, ALU.mult).then_inc(d_qm, 1)

            def d_query_out(k):
                if k < NS:
                    if k >= 2:
                        ve.wait_ge(pst_ready, 4 * (k - 1))
                    ve.wait_ge(d_qb, k + 1)
                    ve.tensor_copy(qb[:, :], PT[:, 1, :]).then_inc(d_end, 1)
                    ve.wait_ge(d_end, k + 1)

            def d_close(k, queries):
                ve.wait_ge(d_v1, k - 1)
                need(ve, d_qb, queries)
                for h in range(H):
                    last = ve.tensor_scalar(tmpD[:, h * P:(h + 1) * P], PD[:, h * P:(h + 1) * P],
                                            coefD[:, k % 2:k % 2 + 1], hmask[:, h:h + 1], ALU.mult, ALU.mult)
                last.then_inc(d_om, 1)

            def d_close_out(k):
                ve.wait_ge(d_cmb, k - 1)
                ve.tensor_tensor(oX[0:TR, :], oX[0:TR, :], PT[0:TR, 1, :], ALU.add).then_inc(d_row, 1)
                ve.wait_ge(d_row, k - 1)

            def d_max(k):
                s = sc[:, (k - 1) % 2]
                link(ve.memset(s[:, NPG, :], -BIG))
                link(ve.tensor_scalar(s[0:32, NPG, :], sNew[0:32, :], selm[0:32, k - 1:k], None, ALU.add))
                ve.tensor_reduce(mpart[:, :], s.rearrange("p a c -> p c a"), X, ALU.max).then_inc(d_mx, 1)

            def d_max_all(k):
                ve.wait_ge(d_mxT, k)
                link(ve.tensor_reduce(mx8[:, :], PT[0:HC, 0, 0:P], X, ALU.max))
                ve.tensor_scalar(mxd[:, :], ident[0:HC, 0:HC], mx8[:, 0:1], None, ALU.mult).then_inc(d_mxd, 1)

            def d_subtract(k):
                s = sc[:, (k - 1) % 2]
                ve.wait_ge(d_mb, k)
                ve.tensor_tensor(s, s, PT[:, 0, 0:HC].unsqueeze(1).to_broadcast([P, NPG + 1, HC]),
                                 ALU.subtract).then_inc(d_sub, 1)

            def d_sum(k):
                s = sc[:, (k - 1) % 2]
                ve.wait_ge(d_exp, k)
                link(ve.tensor_reduce(psums[:, :], s.rearrange("p a c -> p c a"), X, ALU.add))
                ve.tensor_copy(srep[:, :].rearrange("p (j c) -> p j c", j=4)[:, :, 0:HC],
                               psums[:, :].unsqueeze(1).to_broadcast([P, 4, HC])).then_inc(d_sr, 1)

            def d_weights(k):
                ve.wait_ge(d_L, k)
                c = coefD[:, (k - 1) % 2:(k - 1) % 2 + 1]
                ve.reciprocal(c, PT[:, 0, 0:1]).then_inc(d_lread, 1)
                ve.wait_ge(d_lread, k)
                link(ve.tensor_tensor(c, c, sgn[:, :], ALU.mult))

            def d_front(k, close=True):
                d_query(k)
                if 1 <= k:
                    d_max(k)
                d_query_out(k)
                if 1 <= k:
                    d_max_all(k)
                if k >= 2 and close:
                    d_close(k, min(k + 1, NS))
                if 1 <= k:
                    d_subtract(k)
                if k >= 2 and close:
                    d_close_out(k)

            def d_back(k):
                if 1 <= k:
                    d_sum(k)
                    d_weights(k)

            ve.wait_ge(norm_in, 16)
            norm_x(0)
            ve.wait_ge(const_in, 16 * 7)
            ve.wait_ge(made, 11)
            for n in range(2):
                link(ve.tensor_tensor(lamr[:, 2 * n, :], lamr[:, 2 * n, :], lamr[:, 2 * n + 1, :], ALU.mult))
                link(ve.tensor_reduce(lamw[:, n:n + 1], lamr[:, 2 * n, :], X, ALU.add))
            ve.tensor_tensor(lbw[:, 0, :], lbl[:, :], lbl[:, :], ALU.subtract).then_inc(cst, 1)
            link(ve.tensor_copy(identb[:, :], ident[:, :]))
            link(ve.tensor_reduce(hmask[:, :], ident[:, :].rearrange("p (j x h c) -> p h x j c", j=4, x=4, c=2)[:, :, 0], XY, ALU.add))
            link(ve.tensor_reduce(sgn[:, :], ident[:, 1:P:2], X, ALU.add))
            link(ve.tensor_scalar(selm[:, :], ident[:, 16:16 + NS], -1.0, BIG, ALU.add, ALU.mult))
            link(ve.tensor_scalar(subw[:, :], subw[:, :], 0.5 * (1.0 - LAM0), None, ALU.mult))
            link(ve.tensor_scalar(hgw[:, :], hgw[:, :], 0.5, None, ALU.mult))
            link(ve.memset(sNew[:, :], 0.0))
            link(ve.memset(oX[:, :], 0.0))
            link(ve.memset(PD[:, :], 0.0))
            for n, (s, v) in enumerate(((k_used, TWO_FREE), (v_used, ONE_ON), (PT_ev, TWO_FREE), (PV_done, TWO_FREE),
                                        (post, FOUR_FREE), (P_tr, ONE_ON), (y_ready, ONE_ON), (x_lev, ONE_ON),
                                        (s_upd, ONE_ON), (yB, ONE_ON), (yT_ev, ONE_ON), (h_add, ONE_ON),
                                        (P_ready, ONE_ON), (a_cp, ONE_ON))):
                ve.memset(start[:, n:n + 1], 0.0).then_inc(s, v)
            ve.wait_ge(lam_e, 2)
            link(ve.tensor_tensor(nlam[:, :], lamw[:, 3:4], lamw[:, 2:3], ALU.subtract))
            link(ve.tensor_scalar(nlam[:, :], nlam[:, :], -LAM0, None, ALU.add))
            link(ve.tensor_scalar(lamw[:, 4:5], nlam[:, :], -1.0, None, ALU.add))
            link(ve.tensor_tensor(lamw[:, 5:6], sgn[:, :], lamw[:, 4:5], ALU.mult))
            link(ve.tensor_scalar(sgn[:, :], lamw[:, 5:6], 1.0, None, ALU.add))
            link(ve.reciprocal(lbw[:, 2, :], lbw[:, 1, :]))
            link(ve.tensor_tensor(lbw[:, 3, :], lbw[:, 1, :], lbw[:, 2, :], ALU.mult))
            link(ve.tensor_tensor(lbw[:, 0, :], lbw[:, 3, :], lbw[:, 3, :], ALU.subtract))
            link(ve.tensor_scalar(lbw[:, 1, :], lbw[:, 0, :], -0.5, 0.5, ALU.mult, ALU.add))
            link(ve.tensor_scalar(lbw[:, 2, :], lbw[:, 1, :], -1.0, None, ALU.mult))
            link(ve.tensor_tensor(lbw[:, 3, :], lbw[:, 0, :], lbw[:, 1, :], ALU.add))
            ve.tensor_copy(mx8[:, :], ones[0:HC, 0:1]).then_inc(cst2, 1)
            ve.wait_ge(proj, 1)
            ve.tensor_copy(U[0:TR, G:D], PS[0:TR, 1, :]).then_inc(k_ev, 1)
            gate(0, gwX[0:TR, :], subw, TR)
            ve.wait_ge(qk_tr, 2)
            ve.wait_ge(made, 12)
            ve.tensor_copy(KT[:, :, NT * P:NT * P + 16], PT[:, 1, 0:H * TR].rearrange("p (h t) -> p h t", h=H)[:, :, 0:16])\
                .then_inc(kT_ev, 1)
            ve.wait_ge(q_ev, 1)
            ve.wait_ge(k_ev, 1)
            link(ve.tensor_tensor(tmpD[0:TR, :], qX[0:TR, :], U[0:TR, G:D], ALU.mult))
            link(ve.tensor_reduce(sNew[0:TR, :], tmpD[0:TR, :].rearrange("p (c d) -> p c d", d=64), X, ALU.add))
            ve.wait_ge(k_st, 32)
            norm_x(1)
            link.flat()

            def post_block(i, it, base, nb, first):
                ve.wait_ge(PV_done, after(base + (i + 1) * nb, TWO_FREE))
                h, c = i // 2, i % 2
                if nb > 1:
                    link(ve.tensor_reduce(rcp[:, 1:2], sums[:, i % 2, 0:nb], X, ALU.add))
                    link(ve.reciprocal(rcp[:, 0:1], rcp[:, 1:2]))
                else:
                    link(ve.reciprocal(rcp[:, 0:1], sums[:, i % 2, 0:1]))
                o = PO[:, (i % OUT_SLOTS) * P:(i % OUT_SLOTS + 1) * P]
                if i == 0:
                    ve.wait_ge(v_st, first)
                if c == 0:
                    ve.tensor_scalar(oh[:, h * P:(h + 1) * P], o, rcp[:, 0:1], None, ALU.mult).then_inc(post, 1)
                else:
                    link(ve.tensor_tensor(rcp[:, 0:1], rcp[:, 0:1], nlam[:, :], ALU.mult))
                    need(ve, post, after(8 * it + i, FOUR_FREE))
                    ve.scalar_tensor_tensor(out=oh[:, h * P:(h + 1) * P], in0=o, scalar=rcp[:, 0:1],
                                            in1=oh[:, h * P:(h + 1) * P], op0=ALU.mult, op1=ALU.add).then_inc(post, 1)

            def row_max(i, it, nb, tail=False, narrow=False):
                ve.wait_ge(S_done, it * 8 + i + 1)
                dst = negm[:, i % 2, 0:1]
                if nb == 1:
                    ve.tensor_reduce(dst, PS[:, i % 2, 0:P if narrow else G], X, ALU.max, negate=True).then_inc(m_ready, 1)
                elif narrow:
                    link(ve.tensor_reduce(dst, PS[:, 0:nb - 1, :], XY, ALU.max, negate=True))
                    link(ve.tensor_reduce(negm[:, i % 2, 1:2], PS[:, nb - 1, 0:P], X, ALU.max, negate=True))
                    ve.tensor_tensor(dst, dst, negm[:, i % 2, 1:2], ALU.min).then_inc(m_ready, 1)
                elif not tail:
                    ve.tensor_reduce(dst, PS[:, 0:nb, :], XY, ALU.max, negate=True).then_inc(m_ready, 1)
                else:
                    link(ve.tensor_reduce(dst, PS[:, :, :], XY, ALU.max, negate=True))
                    link(ve.tensor_reduce(negm[:, i % 2, 1:2], PD[:, 0:16], X, ALU.max, negate=True))
                    ve.tensor_tensor(dst, dst, negm[:, i % 2, 1:2], ALU.min).then_inc(m_ready, 1)

            def head_norm(out, src, src_ready, value, gates, r4, after, rows=P, inc=True):
                ve.wait_ge(src_ready, value)
                rsqrt(r4, ssO[0:rows, :], 1.0 / P)
                for h in range(H):
                    last = ve.scalar_tensor_tensor(out=out[:, h * P:(h + 1) * P], in0=src[:, h * P:(h + 1) * P],
                                                   scalar=r4[:, h:h + 1], in1=gates[:, h * P:(h + 1) * P],
                                                   op0=ALU.mult, op1=ALU.mult)
                last.then_inc(after, 1)

            def a_tile(it, g, r):
                n = it + 1
                nb = g + 1
                base = blocks_before(g, r)
                opening = isinstance(r, int)
                if opening:
                    d_front(g)
                key_slot(it, 0, g)
                key_slot(it, 1, g)
                ve.wait_ge(proj, 4 * n + 1)
                ve.tensor_copy(U[:, G:D], PS[:, 1, :]).then_inc(k_ev, 1)
                if opening:
                    d_back(g)
                early, late = ((2, 3, 4), (5, 6)) if g == 0 else ((2,), (3,))
                for key in early:
                    key_slot(it, key, g)
                gate(n, gw[:, :], subw)
                ve.wait_ge(qk_tr, 2 * n + 2)
                ve.tensor_copy(KT[:, :, bass.ds(it * P, P)], PT[:, 1, :].rearrange("p (h t) -> p h t", h=H)).then_inc(kT_ev, 1)
                for key in late:
                    key_slot(it, key, g)
                for i in range(8):
                    row_max(i, it, nb, narrow=opening)
                    if i >= 1:
                        post_block(i - 1, it, base, nb, 32 * it + 48)
                    if i % 2 and g > 0:
                        key_slot(it, 4 + i // 2, g)
                    if i == 4:
                        ve.wait_ge(k_st, 32 + 16 * (it + 1))
                        norm_x(n + 1)
                post_block(7, it, base, nb, 32 * it + 48)
                if g == 0:
                    key_slot(it, 7, g)
                head_norm(oh, oh, ssO_ready, it + 1, gw, rs, y_ready)

            for g in range(4):
                link.flat()
                a_tile(4 * g, g, 0)
                link.flat()
                link.enter(1, 1 + SLOTS + 8 * (2 if g else 1) + 4 + 2 * RS_STEPS)
                with ve.Fori(1, 4) as r:
                    link.r = r
                    a_tile(4 * g + r, g, r)
                link.leave(3)
            base = blocks_before(4, 0)
            d_close(4, 4)
            for i in range(8):
                row_max(i, NT, 5, tail=True)
                if i == 0:
                    d_close_out(4)
                if i >= 1:
                    post_block(i - 1, NT, base, 5, 32 * NT + 32)
            post_block(7, NT, base, 5, 32 * NT + 32)
            ve.wait_ge(post, after(8 * NT + 8, FOUR_FREE))
            link(ve.tensor_copy(oX[0:16, :], oh[0:16, :]))
            link.flat()

            def forget(cols):
                for h in range(H):
                    a = slice(h * cols, (h + 1) * cols)
                    last = ve.tensor_scalar(kT[:, a], PP[:, a], lbw[:, 2, h:h + 1], lbw[:, 1, h:h + 1], ALU.mult, ALU.add)
                link(last)
                for h in range(H):
                    a = slice(h * cols, (h + 1) * cols)
                    last = ve.tensor_scalar(PP[:, a], PP[:, a], lbw[:, 1, h:h + 1], lbw[:, 3, h:h + 1], ALU.mult, ALU.add)
                last.then_inc(kf, 1)

            def halves(ap, m):
                return ap.rearrange("p (j two m) -> p j two m", two=2, m=m)

            def add_residual(t, rows=P):
                ve.wait_ge(h_mm, t + 1)
                ve.wait_ge(hx_load, 32 * (t + 1))
                hv = hbuf[0:rows, :].rearrange("p (a n) -> p a n", a=2)
                ve.tensor_tensor(hv, hv, PS[0:rows, 0:2, :], ALU.add).then_inc(h_add, 1)

            def final_norm(t, rows=P):
                ve.wait_ge(ssH, t + 1)
                rsqrt(rs[0:rows, 0:1], ssx[0:rows, 1:2], 1.0 / D)
                ve.scalar_tensor_tensor(out=hbuf[0:rows, :], in0=hbuf[0:rows, :], scalar=rs[0:rows, 0:1], in1=fw[0:rows, :],
                                        op0=ALU.mult, op1=ALU.mult).then_inc(y_out, 1)

            def b_tile(t, g, first=False):
                it = t + NT
                n = t + KALL
                opening = isinstance(t, int)
                if opening:
                    d_front(g, close=g > 4)
                if first:
                    ve.wait_ge(PV_done, after(base + 40, TWO_FREE))
                    ve.tensor_copy(masks[:, 0, :], ident[:, :]).then_inc(b_init, 1)
                    ve.wait_ge(b_made, 24)
                    ve.wait_ge(b_init, 1)
                key_slot(it, 0, g)
                if not first:
                    head_norm(ycat[:, 0:G], PO[:, :], ssR, t, gw, rs, yB)
                ve.wait_ge(proj, 4 * n + 1)
                ve.tensor_copy(U[:, G:D], PS[:, 1, :]).then_inc(k_ev, 1)
                if opening:
                    d_back(g)
                key_slot(it, 1, g)
                key_slot(it, 2, g)
                link(ve.memset(QQ, 1.0))
                if not opening:
                    key_slot(it, 3, g)
                gate(n, gw[:, :], hgw)
                ve.wait_ge(z_ev, t + 1)
                forget(P)
                if not opening:
                    key_slot(it, 4, g)
                    key_slot(it, 5, g)
                ve.wait_ge(kf, t + 1)
                ve.wait_ge(qT_ev, n)
                if opening:
                    key_slot(it, 3, g)
                for l in range(8):
                    if l >= 1:
                        m = 1 << (l - 1)
                        xl, q, k, p_, q_ = (halves(a, m) for a in (Xl[l % 2], qT, kT, PP, QQ))
                        if l >= 3:
                            ve.wait_ge(a_lev, 8 * t + (l - 1))
                        ve.tensor_tensor(xl[:, :, 1, :], q[:, :, 1, :], p_[:, :, 1, :], ALU.mult)
                        ve.tensor_tensor(xl[:, :, 0, :], k[:, :, 0, :], q_[:, :, 0, :], ALU.mult).then_inc(x_lev, 1)
                        shape = [P, 4 * P // (2 * m), m]
                        link(ve.tensor_tensor(q_[:, :, 0, :], q_[:, :, 0, :], p_[:, :, 1, m - 1:m].to_broadcast(shape), ALU.mult))
                        link(ve.tensor_tensor(p_[:, :, 1, :], p_[:, :, 1, :], p_[:, :, 0, m - 1:m].to_broadcast(shape), ALU.mult))
                        if l < 7:
                            predicated(ve, l - 1, t, a_lev, a_cp, Am, masks, PS, mpart)
                    if l == 1:
                        key_slot(it, 4 if opening else 6, g)
                    if l == 3 and opening:
                        key_slot(it, 5, g)
                    if l == 2:
                        norm_x(n + 1)
                    if l == 5 and opening:
                        key_slot(it, 6, g)
                ve.tensor_tensor(XQ, qT, PP, ALU.mult)
                ve.tensor_tensor(XK, kT, QQ, ALU.mult).then_inc(x_lev, 1)
                predicated(ve, 6, t, a_lev, a_cp, Am, masks, PS, mpart)
                predicated(ve, 7, t, a_lev, a_cp, Am, masks, PS, mpart)
                if not first:
                    add_residual(t - 1)
                ve.wait_ge(su, t + 1)
                ve.wait_ge(o_done, t + 1)
                for h in range(H):
                    a = slice(h * P, (h + 1) * P)
                    last = ve.scalar_tensor_tensor(out=S_[:, a], in0=S_[:, a], scalar=PP[:, h * P + P - 1:h * P + P],
                                                   in1=PS[:, SU_BANK, a], op0=ALU.mult, op1=ALU.add)
                last.then_inc(s_upd, 1)
                key_slot(it, 7, g)
                if not first:
                    final_norm(t - 1)

            for g in range(4, 8):
                b_tile(4 * (g - 4), g, first=(g == 4))
                link.flat()
                link.enter(1, 1 + SLOTS + 2 + 2 * 7 + 3 * RS_STEPS)
                with ve.Fori(1, 4) as r:
                    link.r = r
                    b_tile(4 * (g - 4) + r, g)
                link.leave(3)
            d_front(8)
            n = 2 * KALL - 1
            head_norm(ycat[:, 0:G], PO[:, :], ssR, NT, gw, rs, yB)
            ve.wait_ge(proj, 4 * n + 1)
            ve.tensor_copy(U[0:TR, G:D], PS[0:TR, 1, :]).then_inc(k_ev, 1)
            d_back(8)
            gate(n, gw[0:TR, :], hgw, TR)
            ve.wait_ge(ssH, NT - 1)
            link(ve.memset(QQ, 1.0))
            link(ve.memset(PTs[:, 0, :], 0.0))
            link(ve.memset(QM, 0.0))
            ve.wait_ge(z_ev, NT + 1)
            forget(TR)
            ve.wait_ge(kf, NT + 1)
            ve.wait_ge(qT_ev, n)
            q3, k3, p3, qq3 = (a[:, 0:H * TR].rearrange("p (h t) -> p h t", h=H) for a in (qT, kT, PP, QQ))
            x3 = [a[:, 0:H * TR].rearrange("p (h t) -> p h t", h=H) for a in Xl]
            link(ve.tensor_copy(fX, p3))
            for h in range(H):
                last = ve.tensor_copy(QM[:, h, 16:16 + 25 * (NS - 1) + 1:25], q3[:, h, 16:TR])
            last.then_inc(t_dve, 1)

            def sub(ap, h, m, half):
                return ap[:, h, 0:16].rearrange("p (j two m) -> p j two m", two=2, m=m)[:, :, half, :]

            for l in range(5):
                if l >= 1:
                    m = 1 << (l - 1)
                    if l >= 3:
                        ve.wait_ge(a_lev, 8 * NT + (l - 1))
                    for h in range(H):
                        ve.tensor_tensor(sub(x3[l % 2], h, m, 1), sub(q3, h, m, 1), sub(p3, h, m, 1), ALU.mult)
                        last = ve.tensor_tensor(sub(x3[l % 2], h, m, 0), sub(k3, h, m, 0), sub(qq3, h, m, 0), ALU.mult)
                    last.then_inc(x_lev, 1)
                    for h in range(H):
                        shape = [P, 16 // (2 * m), m]
                        link(ve.tensor_tensor(sub(qq3, h, m, 0), sub(qq3, h, m, 0), sub(p3, h, m, 1)[:, :, m - 1:m].to_broadcast(shape), ALU.mult))
                        link(ve.tensor_tensor(sub(p3, h, m, 1), sub(p3, h, m, 1), sub(p3, h, m, 0)[:, :, m - 1:m].to_broadcast(shape), ALU.mult))
                    tail_predicated(ve, l - 1, a_lev, a_cp, AX, masks, PS)
            ve.tensor_tensor(qPX[:, :, 0:16], q3[:, :, 0:16], p3[:, :, 0:16], ALU.mult)
            xk3 = XK[:, 0:H * TR].rearrange("p (h t) -> p h t", h=H)
            ve.tensor_tensor(xk3[:, :, 0:16], k3[:, :, 0:16], qq3[:, :, 0:16], ALU.mult).then_inc(x_lev, 1)
            tail_predicated(ve, 4, a_lev, a_cp, AX, masks, PS)
            add_residual(NT - 1)
            final_norm(NT - 1)
            ve.wait_ge(t_act, 2)
            ve.wait_ge(st_in, 16)

            def own_key(b):
                if b >= 2:
                    ve.wait_ge(t_pe, b)
                link(ve.tensor_scalar(kmX[b % 2][0:TR, :], kX[0:TR, :], ident[0:TR, 16 + b:17 + b], None, ALU.mult))
                ve.nop().then_inc(bconst, 1)

            own_key(0)
            for b in range(NS):
                if b + 1 < NS:
                    own_key(b + 1)
                ve.wait_ge(t_pe, b + 2)
                for h in range(H):
                    sx = SX[:, b * H + h, :]
                    last = ve.scalar_tensor_tensor(out=sx, in0=sx, scalar=fX[:, h, 16 + b:17 + b],
                                                   in1=PS[:, 2 + b % 2, h * P:(h + 1) * P], op0=ALU.mult, op1=ALU.add)
                link(last)
            ve.nop().then_inc(t_dve, 1)
            ve.wait_ge(su, NT + 1)
            ve.wait_ge(o_done, NT + 1)
            for h in range(H):
                a = slice(h * P, (h + 1) * P)
                last = ve.scalar_tensor_tensor(out=S_[:, a], in0=S_[:, a], scalar=p3[:, h, 15:16],
                                               in1=PS[:, 0, a], op0=ALU.mult, op1=ALU.add)
            link(last)
            ve.nop().then_inc(t_dve, 2)
            ve.wait_ge(y_tr, 2 * NT)
            head_norm(ycat[0:TR, 0:G], PO[0:TR, :], ssR, NT + 1, gw[0:TR, :], rs[0:TR, :], yB, TR)
            d_close(9, NS)
            d_close_out(9)
            ve.nop().then_inc(t_dve, 1)
            head_norm(ycat[0:TR, G:D], oX[0:TR, :], ssR, NT + 2, gwX[0:TR, :], rs[0:TR, :], yB, TR)
            add_residual(NT, TR)
            final_norm(NT, TR)

        @block.tensor
        def _(pe):
            def x_front(n, half):
                if half == 0:
                    pe.wait_ge(xn_ready, n + 1)
                for c in range(4):
                    mm = pe.transpose(PT[:, half, c * P:(c + 1) * P], U[:, (4 * half + c) * P:(4 * half + c + 1) * P], ident[:, :])
                mm.then_inc(x_tr, 1)

            def project_half(n, b, half, rows=P):
                pe.wait_ge(xT_ready, 2 * n + 2)
                for c in range(4 * half, 4 * half + 4):
                    mm = pe.matmul(PS[0:rows, BANK[b], :], xT[:, c, 0:rows], W[:, b, c, :], start=(c == 0), stop=(c == DC - 1))
                if half:
                    mm.then_inc(proj, 1)

            def project(n, order, rows=P, loaded=None):
                for b in order:
                    if loaded is not None:
                        pe.wait_ge(loaded[b], 16)
                    pe.wait_ge(xT_ready, 2 * n + 2)
                    for c in range(DC):
                        mm = pe.matmul(PS[0:rows, BANK[b], :], xT[:, c, 0:rows], W[:, b, c, :], start=(c == 0), stop=(c == DC - 1))
                    mm.then_inc(proj, 1)

            def qk_transposes(n, rows=P):
                pe.wait_ge(q_ev, n + 1)
                pe.wait_ge(k_ev, n + 1)
                for a in range(2):
                    for h in range(H):
                        mm = pe.transpose(PT[:, a, h * rows:(h + 1) * rows], U[0:rows, (4 * a + h) * P:(4 * a + h + 1) * P],
                                          ident[0:rows, 0:rows])
                    mm.then_inc(qk_tr, 1)

            def turn(i, j, base, nb, tail=False, narrow=False):
                n = i * nb + j
                pe.wait_ge(P_ready, after(base + (n + 1), ONE_ON))
                need(pe, PT_ev, after(base + (n - 1), TWO_FREE))
                if tail and j == 4:
                    mm = pe.transpose(PT[0:16, n % 2, 0:P], P4[:, :], ident[:, :])
                else:
                    place = i % 2 if nb == 1 else j
                    for u in range(1 if narrow and j == nb - 1 else 4):
                        mm = pe.transpose(PT[:, n % 2, u * P:(u + 1) * P], Pb[:, place, u * P:(u + 1) * P], ident[:, :])
                mm.then_inc(P_tr, 1)

            def scores(i, it, base, nb, g, r, tail=False):
                h, c = i // 2, i % 2
                narrow = not tail and isinstance(r, int)
                q = Qz[:, c, h, :]
                if nb == 1:
                    if i >= 2:
                        pe.wait_ge(P_ready, after(base + (i - 1), ONE_ON))
                    w = P if narrow else G
                    pe.matmul(PS[:, i % 2, 0:w], q, KT[:, h, 0:w], start=True, stop=False)
                    pe.matmul(PS[:, i % 2, 0:w], identb[:, :], causal[:, bass.ds(r * (-P) + 384, w)],
                              start=False, stop=True).then_inc(S_done, 1)
                    return
                for j in range(nb):
                    if i and j == nb - 1:
                        turn(i - 1, 0, base, nb, tail, narrow)
                    if i:
                        pe.wait_ge(P_ready, after(base + ((i - 1) * nb + j + 1), ONE_ON))
                    if tail and j == 4:
                        if i == 0:
                            pe.wait_ge(d_om, 3)
                        mm = pe.matmul(PD[:, 0:16], q, KT[:, h, NT * P:NT * P + 16], start=True, stop=False)
                        mm = pe.matmul(PD[:, 0:16], identb[:, :], causal[:, 384:400], start=False, stop=True)
                    else:
                        diag = not tail and j == nb - 1
                        w = P if narrow and diag else G
                        mm = pe.matmul(PS[:, j, 0:w], q, KT[:, h, j * G:j * G + w], start=True, stop=not diag)
                        if diag:
                            mm = pe.matmul(PS[:, j, 0:w], identb[:, :], causal[:, bass.ds(r * (-P) + 384, w)], start=False, stop=True)
                mm.then_inc(S_done, 1)

            def values(i, it, base, nb, tail=False, narrow=False):
                h = i // 2
                slot = i % OUT_SLOTS

                def add(j):
                    n = i * nb + j
                    pe.wait_ge(PT_ev, after(base + (n + 1), TWO_FREE))
                    if j == 0:
                        pe.wait_ge(post, after(8 * it + i, FOUR_FREE))
                    out = PO[:, slot * P:(slot + 1) * P]
                    if tail and j == 4:
                        mm = pe.matmul(out, PTs[0:16, n % 2, 0:P], vX[0:16, h * P:(h + 1) * P], start=False, stop=True)
                    else:
                        count = 1 if narrow and j == nb - 1 else 4
                        for u in range(count):
                            mm = pe.matmul(out, PTs[:, n % 2, u * P:(u + 1) * P], V[:, 4 * j + u, h * P:(h + 1) * P],
                                           start=(j == 0 and u == 0), stop=(j == nb - 1 and u == count - 1))
                    mm.then_inc(PV_done, 1)

                for j in range(nb):
                    if j + 1 < nb:
                        turn(i, j + 1, base, nb, tail, narrow)
                    add(j)

            def value_quad(it, s, g):
                if g == 0:
                    return
                if s == 0:
                    pe.wait_ge(pst_ready, it + (-3))
                ring = Vt
                for half in range(2):
                    if g < 8:
                        pe.wait_ge(v_load[half], (it * 4 + (s // 2 + 1 - 16)) * 32)
                    elif s // 2 % 2 == 0:
                        pe.wait_ge(v_load[half], (28 * 4 + (it - 2 * NT) * 2 + s // 4 + 1) * 32)
                    else:
                        ring = Kt
                        pe.wait_ge(k_load[half], (32 * 4 + (it - 2 * NT) * 2 + s // 4 + 1) * 32)
                for j in range(4):
                    mm = pe.matmul(PD[32 * j:32 * j + HC, :], pst[:, (2 * s + j) * HC:(2 * s + j + 1) * HC], ring[:, j // 2, j % 2, :],
                                   start=False, stop=False, skip_group_check=True)
                mm.then_inc(v_used, 1)

            def d_query(k):
                if k < NS:
                    pe.wait_ge(d_qm, k + 1)
                    pe.matmul(PT[:, 1, :], ones[0:TR, :], tmpD[0:TR, :], start=True, stop=True).then_inc(d_qb, 1)

            def d_close(k):
                for j in range(4):
                    mm = pe.matmul(PD[32 * j:32 * j + HC, :], zero8[0:TR, :], vX[0:TR, :], start=False, stop=True,
                                   skip_group_check=True)
                mm.then_inc(d_v1, 1)

            def own_row(b):
                return pick[:, TR - 1 - NMETA - b:2 * TR - 1 - NMETA - b]

            def d_combine(k):
                pe.wait_ge(d_om, k - 1)
                pe.wait_ge(d_end, min(k + 1, NS))
                pe.matmul(PT[0:TR, 1, :], own_row(k - 2), tmpD[:, :], start=True, stop=True).then_inc(d_cmb, 1)

            def d_max(k):
                pe.wait_ge(d_mx, k)
                pe.transpose(PT[0:HC, 0, 0:P], mpart[:, :], ident[:, :]).then_inc(d_mxT, 1)

            def d_max_spread(k):
                pe.wait_ge(d_mxd, k)
                pe.matmul(PT[:, 0, 0:HC], ones[0:HC, :], mxd[:, :], start=True, stop=True).then_inc(d_mb, 1)

            def d_open(k):
                pe.wait_ge(d_exp, k)
                s = sc[:, (k - 1) % 2]
                for j in range(4):
                    w = s[0:TR, NPG, :] if j == 0 else zero8[0:TR, :]
                    pe.matmul(PD[32 * j:32 * j + HC, :], w, vX[0:TR, :], start=True, stop=False, skip_group_check=True)

            def d_sum(k):
                pe.wait_ge(d_sr, k)
                pe.matmul(PT[:, 0, 0:1], srep[:, :], ones[:, 0:1], start=True, stop=True).then_inc(d_L, 1)

            def opening_front(n, k, rows=P, close=True):
                close = close and k >= 2
                project_half(n, 1, 0, rows)
                project_half(n, 1, 1, rows)
                d_query(k)
                if close:
                    d_close(k)
                project_half(n, 0, 0, rows)
                if k >= 1:
                    d_max(k)
                project_half(n, 0, 1, rows)
                if k >= 1:
                    d_max_spread(k)
                if n > KALL:
                    pe.wait_ge(s_upd, after(n - KALL, ONE_ON))
                project_half(n, 3, 0, rows)
                if close:
                    d_combine(k)
                project_half(n, 3, 1, rows)
                if k >= 1:
                    d_open(k)
                    value_quad(n - 1, 0, k)
                    d_sum(k)
                    pe.wait_ge(d_lread, k)
                if close:
                    pe.wait_ge(d_row, k - 1)
                if k < NS:
                    pe.wait_ge(d_end, k + 1)

            pe.wait_ge(made, 10)
            x_front(0, 0)
            x_front(0, 1)
            project(0, (1, 0, 3, 2), TR, wA)
            pe.wait_ge(k_ev, 1)
            for h in range(H):
                mm = pe.transpose(PT[:, 1, h * TR:(h + 1) * TR], U[0:TR, (4 + h) * P:(5 + h) * P], ident[0:TR, 0:TR])
            mm.then_inc(qk_tr, 2)
            pe.wait_ge(q_ev, 1)
            pe.wait_ge(v_ev, 1)
            pe.wait_ge(g_ev, 1)
            pe.wait_ge(kT_ev, 1)
            pe.wait_ge(cst2, 1)
            x_front(1, 0)
            x_front(1, 1)

            def a_tile(it, g, r):
                n = it + 1
                nb = g + 1
                base = blocks_before(g, r)
                narrow = isinstance(r, int)
                need(pe, P_ready, after(base + 0, ONE_ON))
                if narrow:
                    pe.wait_ge(PT_ev, after(base, TWO_FREE))
                    opening_front(n, g)
                else:
                    project(n, (1, 0, 3))
                    value_quad(it, 0, g)
                    pe.wait_ge(PT_ev, after(base, TWO_FREE))
                qk_transposes(n)
                project_half(n, 2, 0)
                if nb == 4:
                    project_half(n, 2, 1)
                pe.wait_ge(qT_ev, n)
                pe.wait_ge(kT_ev, n + 1)
                pe.wait_ge(g_ev, n + 1)
                if nb == 4:
                    pe.wait_ge(v_ev, n + 1)
                scores(0, it, base, nb, g, r)
                if nb < 4:
                    project_half(n, 2, 1)
                if nb == 1:
                    scores(1, it, base, nb, g, r)
                pe.wait_ge(v_ev, n + 1)
                for i in range(1, 8):
                    if nb == 1:
                        turn(i - 1, 0, base, nb, narrow=narrow)
                        if i < 7:
                            scores(i + 1, it, base, nb, g, r)
                    else:
                        scores(i, it, base, nb, g, r)
                    values(i - 1, it, base, nb, narrow=narrow)
                    if i in (2, 4, 6):
                        value_quad(it, i, g)
                pe.wait_ge(PT_ev, after(base + 7 * nb, TWO_FREE))
                x_front(n + 1, 0)
                x_front(n + 1, 1)
                pe.wait_ge(xT_ready, 2 * n + 4)
                turn(7, 0, base, nb, narrow=narrow)
                values(7, it, base, nb, narrow=narrow)

            for g in range(4):
                a_tile(4 * g, g, 0)
                with pe.Fori(1, 4) as r:
                    a_tile(4 * g + r, g, r)
            base = blocks_before(4, 0)
            pe.wait_ge(P_ready, after(base, ONE_ON))
            pe.wait_ge(PT_ev, after(base, TWO_FREE))
            for h in range(H):
                mm = pe.transpose(PT[:, 0, h * TR:(h + 1) * TR], qX[0:TR, h * P:(h + 1) * P], ident[0:TR, 0:TR])
            mm.then_inc(qX_tr, 1)
            d_close(4)
            pe.wait_ge(qT_ev, NT + 1)
            pe.wait_ge(P_ready, after(base, ONE_ON))
            pe.wait_ge(post, after(8 * NT, FOUR_FREE))
            scores(0, NT, base, 5, 4, 0, tail=True)
            pe.matmul(PT[0:TR, 1, :], own_row(2), tmpD[:, :], start=True, stop=True).then_inc(d_cmb, 1)
            pe.wait_ge(d_row, 3)
            for i in range(1, 8):
                scores(i, NT, base, 5, 4, 0, tail=True)
                values(i - 1, NT, base, 5, tail=True)
            turn(7, 0, base, 5, tail=True)
            values(7, NT, base, 5, tail=True)

            pe.wait_ge(post, after(8 * NT + 8, FOUR_FREE))
            pe.wait_ge(P_ready, after(base + 40, ONE_ON))
            pe.wait_ge(PT_ev, after(base + 40, TWO_FREE))
            pe.wait_ge(wB, 64)
            def y_transposes(t, rows=P):
                pe.wait_ge(yB, after(t + 1, ONE_ON))
                for a in range(2):
                    for c in range(4):
                        mm = pe.transpose(PT[:, a, c * rows:(c + 1) * rows], ycat[0:rows, (4 * a + c) * P:(4 * a + c + 1) * P],
                                          ident[0:rows, 0:rows])
                    mm.then_inc(y_tr, 1)

            def out_quarter(t, quarter, rows=P):
                if quarter == 0:
                    pe.wait_ge(yT_ev, after(2 * t + 2, ONE_ON))
                    pe.wait_ge(wO, 32)
                b = quarter // 2
                for c in range(4 * (quarter % 2), 4 * (quarter % 2) + 4):
                    mm = pe.matmul(PS[0:rows, b, :], yTs[:, c, 0:rows], Wo[:, c, b * G:(b + 1) * G], start=(c == 0), stop=(c == DC - 1))
                if quarter == 3:
                    mm.then_inc(h_mm, 1)

            def b_tile(t, g, first=False):
                it = t + NT
                n = t + KALL
                if not first:
                    pe.wait_ge(h_add, after(t - 1, ONE_ON))
                if isinstance(t, int):
                    opening_front(n, g, close=g > 4)
                else:
                    project(n, (1, 0))
                    pe.wait_ge(s_upd, after(t + 0, ONE_ON))
                    project(n, (3,))
                    value_quad(it, 0, g)
                qk_transposes(n)
                project(n, (2,))
                pe.wait_ge(g_ev, n + 1)
                pe.wait_ge(kf, t + 1)
                pe.wait_ge(qT_ev, n)
                for l in range(8):
                    if l == 1:
                        pe.wait_ge(v_ev, n + 1)
                    if l >= 2:
                        pe.wait_ge(a_cp, after(8 * t + (l - 1), ONE_ON))
                    if l >= 1:
                        pe.wait_ge(x_lev, after(8 * t + l, ONE_ON))
                    for h in range(H):
                        a = slice(h * P, (h + 1) * P)
                        lhs, rhs = (kT[:, a], qT[:, a]) if l == 0 else (Xl[l % 2][:, a], Xl[l % 2][:, a])
                        mm = pe.matmul(PS[:, 2 + l % 2, a], lhs, rhs, start=True, stop=True)
                    mm.then_inc(a_lev, 1)
                    if l == 0 and not first:
                        pe.wait_ge(ya_load, 16 * t)
                        pe.wait_ge(z_ev, t + 1)
                        y_transposes(t - 1)
                    if l in (1, 2, 3, 5) and not first:
                        out_quarter(t - 1, (1, 2, 3, 5).index(l))
                    if l == 4:
                        x_front(n + 1, 0)
                        x_front(n + 1, 1)
                    if l in (1, 4, 7):
                        value_quad(it, {1: 2, 4: 4, 7: 6}[l], g)
                pe.wait_ge(x_lev, after(8 * t + 8, ONE_ON))
                pe.wait_ge(xT_ready, 2 * n + 3)
                for h in range(H):
                    a = slice(h * P, (h + 1) * P)
                    mm = pe.transpose(PT[:, 0, a], XK[:, a], ident[:, :])
                mm.then_inc(kd_tr, 1)
                pe.wait_ge(a_cp, after(8 * t + 8, ONE_ON))
                need(pe, s_upd, after(t + 0, ONE_ON))
                need(pe, yB, after(t + 0, ONE_ON))
                for h in range(H):
                    a = slice(h * P, (h + 1) * P)
                    pe.matmul(PO[:, a], Am[:, a], ib[:, a], start=True, stop=False)
                    mm = pe.matmul(PO[:, a], XQ[:, a], S_[:, a], start=False, stop=True)
                mm.then_inc(o_done, 1)
                pe.wait_ge(kd_ev, t + 1)
                for h in range(H):
                    a = slice(h * P, (h + 1) * P)
                    mm = pe.matmul(PS[:, SU_BANK, a], kd[:, a], ib[:, a], start=True, stop=True)
                mm.then_inc(su, 1)

            for g in range(4, 8):
                b_tile(4 * (g - 4), g, first=(g == 4))
                with pe.Fori(1, 4) as r:
                    b_tile(4 * (g - 4) + r, g)
            n = 2 * KALL - 1
            pe.wait_ge(h_add, after(NT - 1, ONE_ON))
            opening_front(n, 8, TR)
            qk_transposes(n, TR)
            project(n, (2,), TR)
            pe.wait_ge(v_ev, n + 1)
            pe.wait_ge(g_ev, n + 1)
            pe.wait_ge(kf, NT + 1)
            pe.wait_ge(qT_ev, n)
            for l in range(5):
                if l >= 2:
                    pe.wait_ge(a_cp, after(8 * NT + (l - 1), ONE_ON))
                if l >= 1:
                    pe.wait_ge(x_lev, after(8 * NT + l, ONE_ON))
                for h in range(H):
                    a = slice(h * TR, h * TR + 16)
                    lhs, rhs = (kT[:, a], qT[:, a]) if l == 0 else (Xl[l % 2][:, a], Xl[l % 2][:, a])
                    mm = pe.matmul(PS[0:16, 2 + l % 2, h * 16:(h + 1) * 16], lhs, rhs, start=True, stop=True)
                mm.then_inc(a_lev, 1)
                if l == 0:
                    pe.wait_ge(ya_load, 16 * NT)
                    pe.wait_ge(z_ev, NT + 1)
                    y_transposes(NT - 1)
                else:
                    out_quarter(NT - 1, l - 1)
                    if l >= 2:
                        value_quad(2 * NT, 2 * l - 2, 8)
            pe.wait_ge(x_lev, after(8 * NT + 5, ONE_ON))
            for h in range(H):
                pe.transpose(PT[0:16, 0, h * P:(h + 1) * P], XK[:, h * TR:h * TR + 16], ident[:, :])
            for h in range(H):
                mm = pe.transpose(PT[0:TR, 1, h * P:(h + 1) * P], kT[:, h * TR:(h + 1) * TR], ident[:, :])
            mm.then_inc(t_pe, 1)
            for b in range(NS):
                pe.wait_ge(bconst, b + 1)
                if b == 0:
                    pe.wait_ge(a_cp, after(8 * NT + 5, ONE_ON))
                for h in range(H):
                    a = slice(h * P, (h + 1) * P)
                    mm = pe.matmul(PS[:, 2 + b % 2, a], kmX[b % 2][0:TR, a], ib[0:TR, a], start=True, stop=True)
                mm.then_inc(t_pe, 1)
                if b % 2 == 0:
                    value_quad(2 * NT + 1, b, 8)
            pe.wait_ge(t_act, 2)
            pe.wait_ge(h_add, after(NT, ONE_ON))
            for h in range(H):
                a = slice(h * P, (h + 1) * P)
                mm = pe.matmul(PS[:, 0, a], kd[0:16, a], ib[0:16, a], start=True, stop=True)
            mm.then_inc(su, 1)
            pe.wait_ge(t_dve, 2)
            pe.wait_ge(yB, after(NT, ONE_ON))
            for h in range(H):
                a = slice(h * P, (h + 1) * P)
                pe.matmul(PO[0:TR, a], AX[0:16, h, :], ib[0:16, a], start=True, stop=False)
                pe.matmul(PO[0:TR, a], qPX[:, h, :], S_[:, a], start=False, stop=False)
                for b in range(NS):
                    mm = pe.matmul(PO[0:TR, a], QM[:, h, b * TR:(b + 1) * TR], SX[:, b * H + h, :], start=False, stop=(b == NS - 1))
            mm.then_inc(o_done, 1)
            with pe.Fori(2 * NT + 2, 2 * NT + 4) as it:
                for s in range(0, SLOTS, 2):
                    value_quad(it, s, 8)
            d_close(9)
            pe.wait_ge(d_om, 8)
            pe.matmul(PT[0:TR, 1, :], own_row(NS - 1), tmpD[:, :], start=True, stop=True).then_inc(d_cmb, 1)
            pe.wait_ge(yB, after(NT + 2, ONE_ON))
            y_transposes(NT, TR)
            for quarter in range(4):
                out_quarter(NT, quarter, TR)


def predicated(ve, l, t, a_lev, a_cp, Am, masks, PS, spare):
    ve.wait_ge(a_lev, 8 * t + (l + 1))
    need(ve, a_cp, after(8 * t + l, ONE_ON))
    ve.tensor_copy(spare[:, l:l + 1], masks[:, 0, 0:1])
    ve.copy_predicated(Am.rearrange("p (h t) -> p h t", h=H),
                       masks[:, l, :].bitcast(U32).unsqueeze(1).to_broadcast([P, H, P]),
                       PS[:, 2 + l % 2, :].rearrange("p (h t) -> p h t", h=H)).then_inc(a_cp, 1)


def tail_predicated(ve, l, a_lev, a_cp, AX, masks, PS):
    ve.wait_ge(a_lev, 8 * NT + (l + 1))
    ve.wait_ge(a_cp, after(8 * NT + l, ONE_ON))
    ve.copy_predicated(AX[0:16, :, 0:16], masks[0:16, l, 0:16].bitcast(U32).unsqueeze(1).to_broadcast([16, H, 16]),
                       PS[0:16, 2 + l % 2, 0:64].rearrange("p (h t) -> p h t", h=H)).then_inc(a_cp, 1)


_INS = ['x_prompt', 'x_sample', 'cache_k', 'cache_v', 'state_hgrn', 'page_table', 'meta_tokens', 'norm_w', 'w_in',
        'w_out', 'lb_logits', 'hgrn_norm_w', 'subln_w', 'lam_q1', 'lam_k1', 'lam_q2', 'lam_k2', 'final_norm_w']
_OUTS = [((1, 2048, 1024), 'float32'), ((8, 1, 1024), 'float32'), ((1, 1, 2064, 4, 128), 'float32'),
         ((1, 1, 2064, 4, 128), 'float32'), ((1, 1, 4, 128, 128), 'float32'), ((1, 8, 1, 4, 128), 'float32'),
         ((1, 8, 1, 4, 128), 'float32'), ((1, 8, 4, 128, 128), 'float32')]


def kernel(**inputs):
    import numpy as _np
    import concourse.bacc as _bacc
    from concourse import mybir as _mybir
    from concourse.bass_utils import run_bass_kernel_spmd as _run

    nc = _bacc.Bacc("TRN2", target_bir_lowering=False, num_devices=1)
    arrays, args = {}, []
    for name in _INS:
        a = _np.ascontiguousarray(inputs[name])
        arrays[f"in_{name}_dram"] = a
        args.append(nc.dram_tensor(f"in_{name}_dram", a.shape, _mybir.dt.from_np(a.dtype), kind="ExternalInput").ap())
    for i, (shape, dtype) in enumerate(_OUTS):
        dt = _mybir.dt.from_np(_np.dtype(dtype))
        args.append(nc.dram_tensor(f"out_{i}_dram", shape, dt, kind="ExternalOutput").ap())
    build(nc, *args)
    r = _run(nc, [arrays], core_ids=[0])
    return tuple(r.results[0][f"out_{i}_dram"] for i in range(len(_OUTS)))
```
